# Optimizing a Trainium2 kernel written in Bass

```python
import math
import jax, jax.numpy as jnp
from jax import lax
import numpy as np

D_MODEL = 1024
BATCH = 1
SEQ = 512
DEPTH = 2

N_A_LAYERS = DEPTH // 2
N_B_LAYERS = DEPTH - N_A_LAYERS
CONV_KERNEL = 31
HEAD_DIM = 64
N_HEADS = D_MODEL // HEAD_DIM
DILATED_GROUPS = ((128, 1), (512, 4), (2048, 16))
N_DGROUPS = len(DILATED_GROUPS)
GROUP_WIDTH = N_HEADS * HEAD_DIM
BLOCK = 128
ROPE_THETA = 10000.0
N_EXPERT_GROUPS = 4
EXPERTS_PER_GROUP = 4
N_EXPERTS = N_EXPERT_GROUPS * EXPERTS_PER_GROUP
TOP_K_INNER = 2
D_EXPERT = D_MODEL // 2
EPS = 1e-6

kernel_name = "yoco_conformer_dilated_attn_hmoe"

def rms_norm(x, g):
    xf = x.astype(jnp.float32)
    y = xf * lax.rsqrt(jnp.mean(xf * xf, axis=-1, keepdims=True) + EPS)
    return (y * g.astype(jnp.float32)).astype(x.dtype)

def layer_norm(x, g, b):
    xf = x.astype(jnp.float32)
    mu = jnp.mean(xf, axis=-1, keepdims=True)
    var = jnp.mean(jnp.square(xf - mu), axis=-1, keepdims=True)
    y = (xf - mu) * lax.rsqrt(var + EPS)
    return (y * g.astype(jnp.float32) + b.astype(jnp.float32)).astype(x.dtype)

def rotary(x):
    S = x.shape[1]
    pos = jnp.arange(S, dtype=jnp.float32)
    inv_freq = ROPE_THETA ** (-jnp.arange(0, HEAD_DIM, 2, dtype=jnp.float32) / HEAD_DIM)
    ang = pos[:, None] * inv_freq[None, :]
    bshape = (1, S) + (1,) * (x.ndim - 3) + (HEAD_DIM // 2,)
    cos = jnp.cos(ang).reshape(bshape).astype(x.dtype)
    sin = jnp.sin(ang).reshape(bshape).astype(x.dtype)
    x1, x2 = jnp.split(x, 2, axis=-1)
    return jnp.concatenate([x1 * cos - x2 * sin, x2 * cos + x1 * sin], axis=-1)

def conformer_conv(h, w_in, b_in, w_dw, b_dw, ln_g, ln_b, w_out, b_out):
    u = h @ w_in + b_in
    a, gate = jnp.split(u, 2, axis=-1)
    u = a * jax.nn.sigmoid(gate)
    u = lax.conv_general_dilated(
        u, w_dw[:, None, :], window_strides=(1,), padding=[(CONV_KERNEL - 1, 0)],
        dimension_numbers=("NWC", "WIO", "NWC"), feature_group_count=D_MODEL) + b_dw
    u = jax.nn.silu(layer_norm(u, ln_g, ln_b))
    return u @ w_out + b_out

def to_phase_blocks(x, dil):
    B, S = x.shape[:2]
    rest = x.shape[2:]
    L = S // dil
    x = jnp.swapaxes(x.reshape((B, L, dil) + rest), 1, 2)
    nb = -(-L // BLOCK)
    x = jnp.pad(x, [(0, 0), (0, 0), (0, nb * BLOCK - L)] + [(0, 0)] * len(rest))
    return x.reshape((B, dil, nb, BLOCK) + rest)

def from_phase_blocks(x, S, dil):
    B = x.shape[0]
    rest = x.shape[4:]
    L = S // dil
    x = x.reshape((B, dil, -1) + rest)[:, :, :L]
    return jnp.swapaxes(x, 1, 2).reshape((B, S) + rest)

def key_blocks(k, dil):
    kb = to_phase_blocks(k, dil)
    prev = jnp.pad(kb[:, :, :-1], [(0, 0), (0, 0), (1, 0), (0, 0), (0, 0), (0, 0)])
    return jnp.concatenate([prev, kb], axis=3)

def shared_kv(x, kv_norm, w_kv):
    h = rms_norm(x, kv_norm)
    B, S, _ = h.shape
    kv = (h @ w_kv).reshape(B, S, 2, N_DGROUPS, N_HEADS, HEAD_DIM)
    k = rotary(kv[:, :, 0])
    v = kv[:, :, 1]
    return [(key_blocks(k[:, :, g], dil), key_blocks(v[:, :, g], dil))
            for g, (_, dil) in enumerate(DILATED_GROUPS)]

def dilated_group_attention(q, k_cat, v_cat, dil, w_phase):
    S = q.shape[1]
    qb = to_phase_blocks(q, dil)
    nb = qb.shape[2]
    s = jnp.einsum("bpnihd,bpnjhd->bpnhij", qb.astype(jnp.float32), k_cat.astype(jnp.float32))
    i = jnp.arange(BLOCK)[:, None]
    j = jnp.arange(2 * BLOCK)[None, :]
    delta = BLOCK + i - j
    band = (delta >= 0) & (delta <= w_phase)
    blk = jnp.arange(nb)[:, None, None]
    valid = band[None] & ((blk > 0) | (j >= BLOCK)[None])
    s = jnp.where(valid[None, None, :, None], s, -jnp.inf)
    lse = jax.nn.logsumexp(s, axis=-1)
    p = jnp.exp(s - lse[..., None])
    o = jnp.einsum("bpnhij,bpnjhd->bpnihd", p.astype(v_cat.dtype), v_cat)
    return from_phase_blocks(o, S, dil), from_phase_blocks(jnp.moveaxis(lse, -1, 3), S, dil)

def dilated_attention(h, w_q, w_o, kv_blocks):
    B, S, _ = h.shape
    q = rotary((h @ w_q).reshape(B, S, N_DGROUPS, N_HEADS, HEAD_DIM)) * (HEAD_DIM ** -0.5)
    outs, lses = [], []
    for g, (window, dil) in enumerate(DILATED_GROUPS):
        k_cat, v_cat = kv_blocks[g]
        o, lse = dilated_group_attention(q[:, :, g], k_cat, v_cat, dil, window // dil)
        outs.append(o)
        lses.append(lse)
    o = jnp.stack(outs, axis=0).astype(jnp.float32)
    wts = jax.nn.softmax(jnp.stack(lses, axis=0), axis=0)
    comb = jnp.sum(wts[..., None] * o, axis=0).astype(h.dtype)
    return comb.reshape(B, S, GROUP_WIDTH) @ w_o

def hierarchical_moe(h, r_grp, r_exp, w_gate, w_up, w_down):
    B, S, D = h.shape
    t = h.reshape(B * S, D)
    p_grp = jax.nn.softmax((t @ r_grp).astype(jnp.float32), axis=-1)
    g_idx = jnp.argmax(p_grp, axis=-1)
    p_top = jnp.take_along_axis(p_grp, g_idx[:, None], axis=1)[:, 0]
    exp_logits = jnp.einsum("td,gde->tge", t, r_exp).astype(jnp.float32)
    sel = jnp.take_along_axis(exp_logits, g_idx[:, None, None], axis=1)[:, 0]
    top_v, top_i = lax.top_k(sel, TOP_K_INNER)
    w_in = jax.nn.softmax(top_v, axis=-1) * p_top[:, None]
    e_idx = g_idx[:, None] * EXPERTS_PER_GROUP + top_i
    gates = jnp.sum(jax.nn.one_hot(e_idx, N_EXPERTS, dtype=jnp.float32) * w_in[..., None], axis=1)
    a = jnp.einsum("td,edf->tef", t, w_gate)
    u = jnp.einsum("td,edf->tef", t, w_up)
    hid = jax.nn.silu(a) * u * gates[:, :, None].astype(t.dtype)
    y = jnp.einsum("tef,efd->td", hid, w_down)
    return y.reshape(B, S, D)

def setup_inputs(seed: int = 0) -> dict:
    key = jax.random.key(seed)
    ks = jax.random.split(key, 24)
    f32 = jnp.float32
    D = D_MODEL

    def nrm(k, shape, fan_in):
        return jax.random.normal(k, shape, f32) * (fan_in ** -0.5)

    def gain(k, shape):
        return 1.0 + 0.05 * jax.random.normal(k, shape, f32)

    def bias(k, shape):
        return 0.02 * jax.random.normal(k, shape, f32)

    return {
        "x": jax.random.normal(ks[0], (BATCH, SEQ, D), f32),
        "a_norm": gain(ks[1], (N_A_LAYERS, D)),
        "a_w_in": nrm(ks[2], (N_A_LAYERS, D, 2 * D), D),
        "a_b_in": bias(ks[3], (N_A_LAYERS, 2 * D)),
        "a_w_dw": nrm(ks[4], (N_A_LAYERS, CONV_KERNEL, D), CONV_KERNEL),
        "a_b_dw": bias(ks[5], (N_A_LAYERS, D)),
        "a_ln_g": gain(ks[6], (N_A_LAYERS, D)),
        "a_ln_b": bias(ks[7], (N_A_LAYERS, D)),
        "a_w_out": nrm(ks[8], (N_A_LAYERS, D, D), D),
        "a_b_out": bias(ks[9], (N_A_LAYERS, D)),
        "kv_norm": gain(ks[10], (D,)),
        "w_kv": nrm(ks[11], (D, 2 * N_DGROUPS * GROUP_WIDTH), D),
        "b_norm": gain(ks[12], (N_B_LAYERS, D)),
        "b_w_q": nrm(ks[13], (N_B_LAYERS, D, N_DGROUPS * GROUP_WIDTH), D),
        "b_w_o": nrm(ks[14], (N_B_LAYERS, GROUP_WIDTH, D), GROUP_WIDTH),
        "ffn_norm": gain(ks[15], (DEPTH, D)),
        "router_group": nrm(ks[16], (DEPTH, D, N_EXPERT_GROUPS), D),
        "router_expert": nrm(ks[17], (DEPTH, N_EXPERT_GROUPS, D, EXPERTS_PER_GROUP), D),
        "w_gate": nrm(ks[18], (DEPTH, N_EXPERTS, D, D_EXPERT), D),
        "w_up": nrm(ks[19], (DEPTH, N_EXPERTS, D, D_EXPERT), D),
        "w_down": nrm(ks[20], (DEPTH, N_EXPERTS, D_EXPERT, D), D_EXPERT),
        "final_norm": gain(ks[21], (D,)),
    }

def reference(x, a_norm, a_w_in, a_b_in, a_w_dw, a_b_dw, a_ln_g, a_ln_b, a_w_out, a_b_out,
              kv_norm, w_kv, b_norm, b_w_q, b_w_o, ffn_norm, router_group, router_expert,
              w_gate, w_up, w_down, final_norm):
    kv_blocks = None
    for l in range(DEPTH):
        if l < N_A_LAYERS:
            h = rms_norm(x, a_norm[l])
            x = x + conformer_conv(h, a_w_in[l], a_b_in[l], a_w_dw[l], a_b_dw[l],
                                   a_ln_g[l], a_ln_b[l], a_w_out[l], a_b_out[l])
        else:
            j = l - N_A_LAYERS
            h = rms_norm(x, b_norm[j])
            x = x + dilated_attention(h, b_w_q[j], b_w_o[j], kv_blocks)
        h = rms_norm(x, ffn_norm[l])
        x = x + hierarchical_moe(h, router_group[l], router_expert[l], w_gate[l], w_up[l], w_down[l])
        if l == N_A_LAYERS - 1:
            kv_blocks = shared_kv(x, kv_norm, w_kv)
    return rms_norm(x, final_norm)


_drawn_inputs = setup_inputs


def setup_inputs(seed=0):
    import zlib

    import numpy as np

    out = dict(_drawn_inputs(seed))
    spreads = {}
    factors = {'kv_norm': 3.571, 'b_norm': 8.0}
    for name, (base, spread) in spreads.items():
        noise = np.random.default_rng([zlib.crc32(name.encode()), seed]).standard_normal(out[name].shape)
        drawn = base * np.exp(spread * noise) if base else spread * noise
        out[name] = __import__('jax').numpy.asarray(drawn.astype(out[name].dtype))
    for name, factor in factors.items():
        out[name] = (out[name] * factor).astype(out[name].dtype)
    return out
```

```python
from contextlib import ExitStack

import concourse.bass as bass
from concourse import mybir

ALU = mybir.AluOpType
ACT = mybir.ActivationFunctionType
AX = mybir.AxisListType.X
F32 = mybir.dt.float32
F32R = mybir.dt.float32r
BF16 = mybir.dt.bfloat16
U16 = mybir.dt.uint16
U32 = mybir.dt.uint32
I32 = mybir.dt.int32

P = 128
D = 1024
T = 512
NT = T // P
KT = D // P
CONV = 31
PAD = CONV - 1
HEAD = 64
NP_HEADS = D // HEAD // 2
NG = 3
E = 16
EG = 4
F = 512
FT = F // P
EPS = 1e-6
MAXC = T // P
XB = 8
SLOTS = E + XB + 2
NOWHERE = 8 * T
BIG = 1e30
NU = 3
POOL_TAPS = 9
NPROD = 2

V_NORM = {"a": 0, "f0": 8, "kv": 16, "q": 24, "f1": 32}
NORM_COLS = 40
PREV, OWN, PHASE, OWN_T, PREV_T, PHASE_T = range(6)
C_BIN, C_BDW, C_LNG, C_LNB, C_WDW = 0, 16, 24, 32, 40
CONV_COLS = C_WDW + KT * CONV


class Steps:

    def __init__(self, eng, sem):
        self.eng, self.sem, self.n, self.base = eng, sem, 0, 0

    def mark(self, ins):
        ins.then_inc(self.sem, 1)
        self.n += 1

    def wait(self, back=0):
        self.eng.wait_ge(self.sem, self.base + self.n - back)

    def step(self, ins):
        self.mark(ins)
        self.wait()

    def enter(self, i, per):
        self.base = i * per + 0
        self.saved, self.per = self.n, per

    def leave(self, trips):
        assert self.n - self.saved == self.per, (self.n - self.saved, self.per)
        self.base = 0
        self.n = self.saved + self.per * trips


class Count:

    def __init__(self, sem, keys, per):
        self.sem = sem
        self.before = {k: sum(per[:i]) for i, k in enumerate(keys)}

    def at(self, key, n):
        return self.before[key] + n


def build_program(nc, a):
    x, out = a["x"], a["out"]
    xn_dram = [nc.dram_tensor(f"xn_dram{l}", (T, D), F32).ap() for l in range(2)]
    y_dram = [nc.dram_tensor(f"y_dram{l}", (2 * T, D), F32).ap() for l in range(2)]
    slot_dram = [nc.dram_tensor(f"slot_dram{l}", (P * SLOTS, 1), U32).ap() for l in range(2)]

    with ExitStack() as ctx:
        def sb(name, shape, dt=F32):
            return ctx.enter_context(nc.sbuf_tensor(name, shape, dt))

        def sem(name):
            return ctx.enter_context(nc.semaphore(name))

        base = (nc.sbuf_base + 63) // 64 * 64

        def at(name, kib, shape, dt=F32):
            return nc.alloc_sbuf_tensor_at(name, shape, dt, offset=base + int(kib * 1024))

        X = at("X", 0, [P, NT, D])
        HT = at("HT", 16, [P, KT, T])
        HTQ = at("HTQ", 32, [P, KT, T])
        WR = at("WR", 48, [P, 6 * 4096])
        WO = at("WO", 144, [P, KT, D])
        SC = at("SC", 176, [P, 7680])
        ident = at("ident_sb", 206, [P, P])
        c16 = at("c16_sb", 206.5, [P, 3 * P], U16)
        vn = at("vn", 207.25, [P, NORM_COLS])
        ss = at("ss", 207.5, [P, NT])
        rstd = at("rstd", 207.53125, [P, NT])
        idle = at("idle", 207.5625, [P, 1])
        tick = at("tick", 207.59375, [P, 1])
        HTh, HTl = at("HTh", 16, [P, KT, T], F32R), at("HTl", 32, [P, KT, T], F32R)
        HQh, HQl = at("HQh", 48, [P, KT, T], F32R), at("HQl", 64, [P, KT, T], F32R)
        wraw = at("wraw", 80, [P, NU, KT * P])
        wh, wl = at("wh", 92, [P, NU, KT * P], F32R), at("wl", 104, [P, NU, KT * P], F32R)
        oT = at("oT", 116, [P, KT, T])
        KQ = at("KQ", 132, [P, 4, NG, T])
        Vs = at("Vs", 156, [P, NG, NT, 2, P])
        rope_ab = at("rope_ab", 168, [P, 4, T])
        Pm2 = at("Pm", 176, [P, 3840])
        QKh = at("QKh", 176, [P, 2, NG, T], F32R)
        masks = at("masks_sb", 191, [P, 6, P], U16)
        rope_t = at("rope_sb", 192.5, [P, 4, T])
        rowt = at("rowt", 200.5, [P, T])
        NM = at("NM", 202.5, [P, 16])
        vT = at("vT", 203.5, [P, T])
        PS = [ctx.enter_context(nc.psum_tensor(f"PS{b}", [P, 512], F32)) for b in range(8)]

        c16b = c16[:, :].bitcast(BF16)
        ident_b, before_b, ones_b = c16b[:, 0:P], c16b[:, P:2 * P], c16b[:, 2 * P:3 * P]
        HTf = HT[:, :, :].rearrange("p a b -> p (a b)")
        HTQf = HTQ[:, :, :].rearrange("p a b -> p (a b)")

        def cut(buf, at, *dims):
            n = 1
            for d in dims:
                n *= d
            ap = buf[:, at:at + n]
            if len(dims) == 2:
                return ap.rearrange("p (a b) -> p a b", a=dims[0])
            if len(dims) == 3:
                return ap.rearrange("p (a b c) -> p a b c", a=dims[0], b=dims[1])
            if len(dims) == 4:
                return ap.rearrange("p (a b c d) -> p a b c d", a=dims[0], b=dims[1], c=dims[2])
            return ap

        XN = {"a": cut(HTQf, 0, NT, D), "f0": cut(HTQf, 0, NT, D), "f1": cut(HTQf, 0, NT, D),
              "kv": cut(SC, 0, NT, D), "out": cut(WR, 0, NT, D)}
        w_in_sb = [cut(WR, b * 2048, KT, 2, P) for b in range(2)]
        b_out_sb = cut(WR, 5 * 4096, D)
        W_U = PAD + T
        upad = [cut(SC, b * W_U, W_U) for b in range(2)]
        o = 2 * W_U
        sig = [cut(SC, o + b * T, T) for b in range(2)]
        o += 2 * T
        accv = [cut(SC, o + b * T, T) for b in range(2)]
        o += 2 * T
        accp = [cut(SC, o + b * T, T) for b in range(2)]
        o += 2 * T
        lnsq = [cut(SC, o + b * T, T) for b in range(2)]
        o += 2 * T
        onesf = cut(SC, o, P)
        o += P
        cv = cut(SC, o, CONV_COLS)
        o += CONV_COLS
        taps_v = [cut(SC, o + b * 32, 32) for b in range(2)]
        o += 64
        ctap = [cut(SC, o + b * T, T) for b in range(NPROD)]
        o += NPROD * T
        lnstd = cut(SC, o, T)
        o += T
        assert o <= 7680 - KT * (EG + E)
        wg = [cut(WR, b * 4096, KT, F) for b in range(2)]
        wu = [cut(WR, (2 + b) * 4096, KT, F) for b in range(2)]
        wd = [cut(WR, (4 + b) * 4096, FT, D) for b in range(2)]
        xg = [cut(SC, b * D, D) for b in range(2)]
        xgT = [cut(SC, 2 * D + b * D, KT, P) for b in range(2)]
        sil = cut(SC, 4096, F)
        hid = cut(SC, 4608, F)
        hidT = cut(SC, 5120, FT, P)
        yst = [cut(SC, 5632 + b * D, D) for b in range(2)]
        rt = cut(SC, 7680 - KT * (EG + E), KT, EG + E)
        yg = [cut(HTf, 0, NT, D), cut(SC, 0, NT, D)]
        o = 0

        def rs(*dims, dt=F32):
            nonlocal o
            n = 1
            for d in dims:
                n *= d
            ap = cut(HTQf, o, *dims)
            o += n
            return ap.bitcast(dt) if dt != F32 else ap

        lg = rs(NT, EG + E)
        gmax, gsum, ptop = rs(NT, 1), rs(NT, 1), rs(NT, 1)
        gexp = rs(NT, EG)
        gsel = rs(NT, EG)
        prod = rs(NT, EG, EG)
        sel = rs(NT, EG)
        top = [rs(NT, 1) for _ in range(2)]
        esel = [rs(NT, EG) for _ in range(2)]
        pick = rs(NT, 1)
        tmp4 = rs(NT, EG)
        hot_all = rs(2 * NT, E)
        hot = [hot_all[:, k * NT:(k + 1) * NT, :].rearrange("p n (g e) -> p n g e", g=EG) for k in range(2)]
        both = cut(HTQf, o, NT * E // 2).bitcast(BF16).rearrange("p (a b) -> p a b", a=NT)
        o += NT * E // 2
        rank = rs(NT, E)
        count = rs(E)
        wt = [rs(NT, 1) for _ in range(2)]
        rk = rs(2 * NT)
        ge = rs(2 * NT, MAXC + 1)
        inblk = rs(2 * NT, MAXC)
        col4 = rs(2 * NT, MAXC)
        col = rs(2 * NT)
        hr = rs(2 * NT, E)
        big = rs(2 * NT, MAXC, E)
        over = rs(MAXC - 1, E)
        pos = rs(MAXC, E)
        nover = rs(1)
        gadd = rs(2 * NT)
        half4 = rs(4)
        match = rs(XB, MAXC - 1, E)
        blk_e = rs(E + XB, dt=I32)
        blk_f = rs(XB)
        npair_i = rs(1, dt=I32)
        slot_addr = rs(2 * NT, dt=U32)
        slot_ids = rs(SLOTS, dt=U32)
        src_ids = rs(SLOTS, dt=U32)
        src_f = rs(SLOTS)
        scol = [rs(1, dt=U32) for _ in range(2)]
        dcol = [rs(1, dt=U32) for _ in range(2)]
        ones48 = rs(MAXC - 1, E)
        limits = rs(MAXC + 1)
        xcols = rs(XB)
        tie_w = rs(EG)
        eidx = rs(E)
        tok = rs(2 * NT, dt=U32)
        zeros_u = cut(WR, 5 * 4096 + 2048, SLOTS).bitcast(U32)
        Kh = [KQ[:, h, :, :] for h in range(2)]
        Qh = [KQ[:, 2 + h, :, :] for h in range(2)]
        Pm = [Pm2[:, h * 1920:(h + 1) * 1920] for h in range(2)]
        masks_b = masks[:, :, :].bitcast(BF16)
        fin_g = cut(WR, 5 * 4096, D)

        x_in = [sem(f"x_in{n}") for n in range(NT)]
        const_in, cvec_in, bout_in, wout_in = sem("const_in"), sem("cvec_in"), sem("bout_in"), sem("wout_in")
        norms = ("a", "f0", "kv", "f1", "out")
        half = KT // 2
        sq_done = Count(sem("sq_done"), norms, [NT] * 5)
        var_ready = Count(sem("var_ready"), norms, [1] * 5)
        std_ready = Count(sem("std_ready"), norms, [1] * 5)
        xn_ready = Count(sem("xn_ready"), norms, [NT] * 5)
        xT_ready = Count(sem("xT_ready"), norms, [KT] * 4 + [0])
        ht_act = Count(sem("ht_act"), norms, [half, half, 2 * KT, half, 0])
        ht_dve = Count(sem("ht_dve"), norms, [half, half, 2 * KT, half, 0])
        x_upd = Count(sem("x_upd"), norms, [0] + [NT] * 4)
        v_steps, p_steps = sem("v_steps"), sem("p_steps")
        win_in = [sem(f"win_in{b}") for b in range(2)]
        u_mm = [sem(f"u_mm{b}") for b in range(2)]
        sig_done = [sem(f"sig_done{b}") for b in range(2)]
        glu_done = [sem(f"glu_done{b}") for b in range(2)]
        pool_conv = [sem(f"pool_conv{b}") for b in range(2)]
        conv_done = [sem(f"conv_done{b}") for b in range(2)]
        bout_added, mean_mm, ln_d, ln_sq, var_mm = (sem(s) for s in ("bout_added", "mean_mm", "ln_d", "ln_sq", "var_mm"))
        lnvar_ready, lnstd_ready, ln_n, silu_done, wout_mm = (sem(s) for s in ("lnvar_ready", "lnstd_ready", "ln_n", "silu_done", "wout_mm"))
        conv_init, prod_done = sem("conv_init"), sem("prod_done")
        L2 = range(2)
        xn_stored = Count(sem("xn_stored"), L2, [NT * 16] * 2)
        rt_in = Count(sem("rt_in"), L2, [16] * 2)
        slots_zeroed = Count(sem("slots_zeroed"), L2, [16] * 2)
        iota_done = Count(sem("iota_done"), L2, [2] * 2)
        xg_idle = Count(sem("xg_idle"), L2, [1] * 2)
        src_ready = Count(sem("src_ready"), L2, [1] * 2)
        logit_mm = Count(sem("logit_mm"), L2, [1] * 2)
        gdiff = Count(sem("gdiff"), L2, [1] * 2)
        gexp_done = Count(sem("gexp_done"), L2, [2] * 2)
        both_ready = Count(sem("both_ready"), L2, [1] * 2)
        rank_mm = Count(sem("rank_mm"), L2, [1] * 2)
        routed = Count(sem("routed"), L2, [1] * 2)
        scattered = Count(sem("scattered"), L2, [2 * NT * 16] * 2)
        slots_in = Count(sem("slots_in"), L2, [16] * 2)
        zero_ready = sem("zero_ready")
        scol_done = [sem(f"scol_done{l}") for l in L2]
        dcol_done = [sem(f"dcol_done{l}") for l in L2]
        gathered = [[sem(f"gathered{l}{b}") for b in range(2)] for l in L2]
        xgT_mm = [[sem(f"xgT_mm{l}{b}") for b in range(2)] for l in L2]
        xgT_done = [[sem(f"xgT_done{l}{b}") for b in range(2)] for l in L2]
        wg_in = [[sem(f"wg_in{l}{b}") for b in range(2)] for l in L2]
        wu_in = [[sem(f"wu_in{l}{b}") for b in range(2)] for l in L2]
        wd_in = [[sem(f"wd_in{l}{b}") for b in range(2)] for l in L2]
        gate_mm = [sem(f"gate_mm{l}") for l in L2]
        up_mm = [sem(f"up_mm{l}") for l in L2]
        hT_mm = [sem(f"hT_mm{l}") for l in L2]
        down_mm = [sem(f"down_mm{l}") for l in L2]
        sil_done = [sem(f"sil_done{l}") for l in L2]
        hid_done = [sem(f"hid_done{l}") for l in L2]
        hidT_done = [sem(f"hidT_done{l}") for l in L2]
        y_done = [sem(f"y_done{l}") for l in L2]
        y_stored = [[sem(f"y_stored{l}{b}") for b in range(2)] for l in L2]
        y_back = [sem(f"y_back{n}") for n in range(NT)]
        att_const = sem("att_const")
        wu_raw = [sem(f"wu_raw{s}") for s in range(NU)]
        wh_done, wl_done, unit_mm, att_init = (sem(s) for s in ("wh_done", "wl_done", "unit_mm", "att_init"))
        pairs_done, row_done = sem("pairs_done"), sem("row_done")
        rope_ab_done, hi_done, oTh_done, oTl_done, o_free = (sem(s) for s in ("rope_ab_done", "hi_done", "oTh_done", "oTl_done", "o_free"))
        rope_done, v_done = (sem(s) for s in ("rope_done", "v_done"))
        s1_mm, max_done, row_mm, vT_done, v_mm = (sem(s) for s in ("s1_mm", "max_done", "row_mm", "vT_done", "v_mm"))
        s2_mm, exp_done, pv_mm, oT_done, wo_mm = (sem(s) for s in ("s2_mm", "exp_done", "pv_mm", "oT_done", "wo_mm"))
        fin_in, y_ready, out_stored = sem("fin_in"), sem("y_ready"), sem("out_stored")

        block = ctx.enter_context(nc.Block())

        @block.sync
        def _(sp):
            for n in range(NT):
                sp.dma_start(X[:, n, :], x[0, n * P:(n + 1) * P, :]).then_inc(x_in[n], 16)
            for b in range(2):
                sp.dma_start(w_in_sb[b].rearrange("p a b c -> p (a b c)"), a["w_in"][b]).then_inc(win_in[b], 16)
            sp.wait_ge(zero_ready, 1)
            for l in L2:
                sp.dma_start(slot_dram[l].rearrange("(p j) o -> p (j o)", j=SLOTS), zeros_u).then_inc(slots_zeroed.sem, 16)
            sp.dma_start(WO[:, :, :], a["w_out"]).then_inc(wout_in, 16)

            def expert_load(l, j, b, dst, name, s):
                src = a[name][bass.ds(j, 1), :, :].rearrange("e p n -> (e p) n") if not isinstance(j, int) else a[name][j]
                sp.dma_start(dst[b].rearrange("p a b -> p (a b)"), src).then_inc(s[l][b], 16)

            expert_load(0, 1, 1, wg, "w_gate", wg_in)
            for b in range(2):
                expert_load(0, b, b, wu, "w_up", wu_in)
            expert_load(0, 0, 0, wd, "w_down", wd_in)
            with sp.Fori(1, KT // 2) as i:
                for b in range(2):
                    sp.wait_ge(u_mm[b], i)
                    sp.dma_start(w_in_sb[b].rearrange("p a b c -> p (a b c)"),
                                 a["w_in"][bass.ds(2 * i + b, 1), :, :].rearrange("e p n -> (e p) n")).then_inc(win_in[b], 16)

            for b in range(2):
                sp.wait_ge(u_mm[b], KT // 2)
            expert_load(0, 0, 0, wg, "w_gate", wg_in)
            sp.wait_ge(bout_added, NT)
            for l in L2:
                sp.wait_ge(slots_zeroed.sem, slots_zeroed.at(l, 16))
            expert_load(0, 1, 1, wd, "w_down", wd_in)

            def moe_sp(l):
                for n in range(NT):
                    sp.wait_ge(xn_ready.sem, xn_ready.at(f"f{l}", n + 1))
                    sp.dma_start(xn_dram[l][n * P:(n + 1) * P, :], XN[f"f{l}"][:, n, :]).then_inc(xn_stored.sem, 16)
                sp.wait_ge(scattered.sem, scattered.at(l, 2 * NT * 16))
                sp.wait_ge(xn_stored.sem, xn_stored.at(l, NT * 16))
                sp.dma_start(slot_ids, slot_dram[l].rearrange("(p j) o -> p (j o)", j=SLOTS)).then_inc(slots_in.sem, 16)
                sp.wait_ge(routed.sem, routed.at(l, 1))
                npair = sp.value_load(npair_i[0:1, 0:1], min_val=E // 2, max_val=(E + XB) // 2)
                with sp.Fori(1, npair) as i:
                    for b in range(2):
                        j = sp.value_load(blk_e[0:1, bass.ds(2 * i + b, 1)], min_val=0, max_val=E - 1) + l * E
                        for dst, name, s, used in ((wg, "w_gate", wg_in, gate_mm), (wu, "w_up", wu_in, up_mm), (wd, "w_down", wd_in, down_mm)):
                            sp.wait_ge(used[l], 2 * i + b - 1)
                            expert_load(l, j, b, dst, name, s)
                for b in range(2):
                    sp.wait_ge(y_stored[l][b], npair * 16)
                sp.wait_ge(xg_idle.sem, xg_idle.at(l, 1))
                for n in range(NT):
                    for k in range(2):
                        sp.dma_start(yg[k][:, n, :], y_dram[l][k * T + n * P:k * T + (n + 1) * P, :]).then_inc(y_back[n], 16)

            moe_sp(0)
            def unit(src, s):
                sp.dma_start(wraw[:, s, :], src).then_inc(wu_raw[s], 16)

            for m in range(NU):
                unit(a["w_qkv"][m], m)
            sp.dma_start(rope_t[:, :, :], a["rope"]).then_inc(att_const, 16)
            sp.wait_ge(xT_ready.sem, xT_ready.at("kv", KT))
            sp.dma_start(masks[:, :, :].rearrange("p a b -> p (a b)"), a["masks"]).then_inc(att_const, 16)
            with sp.Fori(0, NP_HEADS - 1) as i:
                for u in range(9):
                    sp.wait_ge(wl_done, 9 * i + (u + 1))
                    unit(a["w_qkv"][bass.ds(9 * i + (u + NU), 1), :, :].rearrange("e p n -> (e p) n"), u % NU)
            for m in range(9 * (NP_HEADS - 1) + NU, 9 * NP_HEADS + KT):
                sp.wait_ge(wl_done, m - NU + 1)
                unit(a["w_qkv"][m] if m < 9 * NP_HEADS else a["w_o"][m - 9 * NP_HEADS], m % NU)
            sp.wait_ge(oT_done, 2 * NP_HEADS)
            sp.dma_start(rt.rearrange("p a b -> p (a b)"), a["router"][1]).then_inc(rt_in.sem, 16)
            sp.wait_ge(wo_mm, 2 * NT)
            for b in range(2):
                expert_load(1, E + b, b, wg, "w_gate", wg_in)
                expert_load(1, E + b, b, wu, "w_up", wu_in)
            expert_load(1, E + 1, 1, wd, "w_down", wd_in)
            expert_load(1, E, 0, wd, "w_down", wd_in)
            moe_sp(1)
            sp.dma_start(fin_g, a["final_norm"].to_broadcast([P, D])).then_inc(fin_in, 16)
            for n in range(NT):
                sp.wait_ge(y_ready, n + 1)
                sp.dma_start(out[0, n * P:(n + 1) * P, :], XN["out"][:, n, :]).then_inc(out_stored, 16)
            sp.wait_ge(out_stored, NT * 16)

        @block.gpsimd
        def _(pool):
            steps = Steps(pool, p_steps)
            nc.gpsimd.memset(zeros_u, NOWHERE).then_inc(zero_ready, 1)
            nc.gpsimd.memset(onesf, 1.0 / D)
            for b in range(2):
                last = nc.gpsimd.memset(upad[b][:, 0:PAD], 0.0)
            last.then_inc(conv_init, 1)
            pool.wait_ge(bout_in, 16)
            for n in range(NT):
                pool.wait_ge(xn_ready.sem, xn_ready.at("a", n + 1))
                nc.gpsimd.tensor_tensor(X[:, n, :], X[:, n, :], b_out_sb, ALU.add).then_inc(bout_added, 1)
            with pool.Fori(0, KT // 2) as i:
                steps.enter(i, 2 * (POOL_TAPS - 2))
                for b in range(2):
                    for t in range(1, POOL_TAPS):
                        pool.wait_ge(prod_done, (2 * i + b) * POOL_TAPS + (t + 1))
                        if t == 1:
                            pool.wait_ge(conv_done[b], i)
                            ins = nc.gpsimd.tensor_tensor(accp[b], ctap[0], ctap[1], ALU.add)
                        else:
                            ins = nc.gpsimd.tensor_tensor(accp[b], accp[b], ctap[t % NPROD], ALU.add)
                        if t < POOL_TAPS - 1:
                            steps.step(ins)
                        else:
                            ins.then_inc(pool_conv[b], 1)
                steps.leave(KT // 2)

            def moe_pool(l):
                pool.wait_ge(xn_stored.sem, xn_stored.at(l, NT * 16))
                pool.wait_ge(xT_ready.sem, xT_ready.at(f"f{l}", KT))
                nc.gpsimd.iota(tok, pattern=[[T, 2], [P, NT]], base=0, channel_multiplier=1).then_inc(iota_done.sem, 1)
                for b in range(2):
                    last = nc.gpsimd.memset(xg[b], 0.0)
                last.then_inc(iota_done.sem, 1)
                pool.wait_ge(iota_done.sem, iota_done.at(l, 2))
                pool.wait_ge(slots_zeroed.sem, slots_zeroed.at(l, 16))
                pool.wait_ge(routed.sem, routed.at(l, 1))
                for c in range(2 * NT):
                    pool.indirect_dma_start(slot_dram[l], bass.IndirectOffsetOnAxis(ap=slot_addr[:, c:c + 1], axis=0),
                                            tok[:, c:c + 1], None).then_inc(scattered.sem, 16)
                npair = pool.value_load(npair_i[0:1, 0:1], min_val=E // 2, max_val=(E + XB) // 2)

                def gather(b, n):
                    pool.wait_ge(gathered[l][b], n * 16)
                    nc.gpsimd.tensor_copy(scol[b], src_ids[:, bass.ds(2 * n + b, 1)]).then_inc(scol_done[l], 1)
                    pool.wait_ge(xgT_mm[l][b], n)
                    pool.wait_ge(scol_done[l], 2 * n + b + 1)
                    nc.gpsimd.tensor_tensor(idle[:, :], ident[:, 0:1], ident[:, 0:1], ALU.mult)
                    pool.indirect_dma_start(xg[b], None, xn_dram[l], bass.IndirectOffsetOnAxis(ap=scol[b], axis=0),
                                            bounds_check=T - 1, oob_is_err=False).then_inc(gathered[l][b], 16)

                def scatter(b, n):
                    pool.wait_ge(y_stored[l][b], n * 16)
                    nc.gpsimd.tensor_copy(dcol[b], slot_ids[:, bass.ds(2 * n + b, 1)]).then_inc(dcol_done[l], 1)
                    pool.wait_ge(y_done[l], 2 * n + b + 1)
                    pool.wait_ge(dcol_done[l], 2 * n + b + 1)
                    nc.gpsimd.tensor_tensor(idle[:, :], ident[:, 0:1], ident[:, 0:1], ALU.mult)
                    pool.indirect_dma_start(y_dram[l], bass.IndirectOffsetOnAxis(ap=dcol[b], axis=0), yst[b], None,
                                            bounds_check=2 * T - 1, oob_is_err=False).then_inc(y_stored[l][b], 16)

                pool.wait_ge(src_ready.sem, src_ready.at(l, 1))
                for b in range(2):
                    gather(b, 0)
                with pool.Fori(0, npair) as i:
                    for b in range(2):
                        gather(b, i + 1)
                    for b in range(2):
                        scatter(b, i)

            moe_pool(0)
            pool.wait_ge(down_mm[0], E)
            for n in range(NT):
                pool.wait_ge(y_back[n], 32)
            steps.step(nc.gpsimd.memset(Vs[:, :, :, :, :], 1.0))
            for h in range(2):
                steps.step(nc.gpsimd.memset(Kh[h][HEAD:HEAD + 1, :, :], 1.0))
            nc.gpsimd.memset(idle[:, :], 0.0).then_inc(att_init, 1)
            with pool.Fori(0, NP_HEADS) as i:
                for t in range(6):
                    dst, g = (Qh, t) if t < 3 else (Kh, t - 3)
                    pool.wait_ge(rope_ab_done, 6 * i + (t + 1))
                    if t == 0:
                        pool.wait_ge(pairs_done, i + 1)
                    for h in range(2):
                        rows = slice(h * HEAD, (h + 1) * HEAD)
                        ins = nc.gpsimd.tensor_tensor(dst[h][0:HEAD, g, :], rope_ab[rows, 2 * (t % 2), :], rope_ab[rows, 2 * (t % 2) + 1, :], ALU.add)
                        ins.then_inc(rope_done, 1)
            moe_pool(1)

        @block.scalar
        def _(act):
            act.dma_start(ident[:, :], a["ident"]).then_inc(const_in, 16)
            act.dma_start(vn[:, :], a["norm_vecs"]).then_inc(const_in, 16)
            act.dma_start(c16[:, :], a["c16"]).then_inc(const_in, 16)
            act.dma_start(cv, a["conv_vecs"]).then_inc(cvec_in, 16)
            act.dma_start(b_out_sb, a["b_out"].to_broadcast([P, D])).then_inc(bout_in, 16)
            act.dma_start(rt.rearrange("p a b -> p (a b)"), a["router"][0]).then_inc(rt_in.sem, 16)

            def norm_act(k):
                for n in range(NT):
                    if k == "a":
                        act.wait_ge(x_in[n], 16)
                    else:
                        act.wait_ge(x_upd.sem, x_upd.at(k, n + 1))
                    nc.scalar.activation(XN[k][:, n, :], X[:, n, :], ACT.Square, accum_out=ss[:, n:n + 1]).then_inc(sq_done.sem, 1)
                act.wait_ge(var_ready.sem, var_ready.at(k, 1))
                nc.scalar.activation(rstd[:, :], ss[:, :], ACT.Sqrt).then_inc(std_ready.sem, 1)
                if k == "out":
                    return
                if k == "kv":
                    for kt in range(KT):
                        act.wait_ge(xT_ready.sem, xT_ready.at(k, kt + 1))
                        for dst, v in ((HTh, V_NORM["kv"]), (HQh, V_NORM["q"])):
                            nc.scalar.activation(dst[:, kt, :], PS[kt][:, :], ACT.Copy, scale=vn[:, v + kt:v + kt + 1]).then_inc(ht_act.sem, 1)
                    return
                for kt in range(KT):
                    if kt % 2 == 0:
                        act.wait_ge(xT_ready.sem, xT_ready.at(k, kt + 1))
                        nc.scalar.activation(HT[:, kt, :], PS[kt][:, :], ACT.Copy, scale=vn[:, V_NORM[k] + kt:V_NORM[k] + kt + 1]).then_inc(ht_act.sem, 1)

            act.wait_ge(const_in, 48)
            norm_act("a")
            act.wait_ge(cvec_in, 16)
            with act.Fori(0, KT // 2) as i:
                for b in range(2):
                    act.wait_ge(u_mm[b], i + 1)
                    act.wait_ge(glu_done[b], i)
                    nc.scalar.activation(sig[b], PS[2 * b + 1][:, :], ACT.Sigmoid,
                                         bias=cv[:, bass.ds(2 * i + b + (C_BIN + KT), 1)]).then_inc(sig_done[b], 1)
                    act.wait_ge(glu_done[b], i + 1)
                    for t in range(POOL_TAPS):
                        if t < NPROD:
                            act.wait_ge(pool_conv[1 - b], i + b)
                        elif t == NPROD:
                            act.wait_ge(p_steps, (2 * i + b) * (POOL_TAPS - 2) + 1)
                        else:
                            act.wait_ge(p_steps, (2 * i + b) * (POOL_TAPS - 2) + (t - NPROD))
                        tap = CONV - POOL_TAPS + t
                        nc.scalar.activation(ctap[t % NPROD], upad[b][:, tap:tap + T], ACT.Copy,
                                             scale=cv[:, bass.ds((2 * i + b) * CONV + (C_WDW + tap), 1)]).then_inc(prod_done, 1)
            for c in range(KT):
                act.wait_ge(ln_d, c + 1)
                if c >= 2:
                    act.wait_ge(var_mm, c - 1)
                nc.scalar.activation(lnsq[c % 2], HTQ[:, c, :], ACT.Square).then_inc(ln_sq, 1)
            act.wait_ge(lnvar_ready, 1)
            nc.scalar.activation(lnstd, lnstd, ACT.Sqrt).then_inc(lnstd_ready, 1)
            for c in range(KT):
                act.wait_ge(ln_n, c + 1)
                nc.scalar.activation(HTQ[:, c, :], HTQ[:, c, :], ACT.Silu, bias=cv[:, C_LNB + c:C_LNB + c + 1],
                                     scale=cv[:, C_LNG + c:C_LNG + c + 1]).then_inc(silu_done, 1)

            def moe_act(l):
                norm_act(f"f{l}")
                act.wait_ge(gdiff.sem, gdiff.at(l, 1))
                nc.scalar.activation(gexp, gexp, ACT.Exp).then_inc(gexp_done.sem, 1)
                nc.scalar.activation(pick, pick, ACT.Exp).then_inc(gexp_done.sem, 1)
                act.wait_ge(routed.sem, routed.at(l, 1))
                npair = act.value_load(npair_i[0:1, 0:1], min_val=E // 2, max_val=(E + XB) // 2)
                with act.Fori(0, npair) as i:
                    def silu_gate(b):
                        act.wait_ge(gate_mm[l], 2 * i + b + 1)
                        act.wait_ge(hid_done[l], 2 * i + b)
                        nc.scalar.activation(sil, PS[0][:, :], ACT.Silu).then_inc(sil_done[l], 1)

                    def store_y(b):
                        act.wait_ge(down_mm[l], 2 * i + b + 1)
                        act.wait_ge(y_stored[l][b], i * 16)
                        nc.scalar.activation(yst[b][:, 0:512], PS[3][:, :], ACT.Copy)
                        nc.scalar.activation(yst[b][:, 512:1024], PS[4][:, :], ACT.Copy).then_inc(y_done[l], 1)

                    silu_gate(0)
                    silu_gate(1)
                    store_y(0)
                    store_y(1)

            moe_act(0)
            norm_act("kv")
            act.wait_ge(att_init, 1)

            def leading(s, n, m, used):
                act.wait_ge(wu_raw[s], n)
                if used is not None:
                    act.wait_ge(unit_mm, used)
                nc.scalar.activation(wh[:, s, :], wraw[:, s, :], ACT.Copy).then_inc(wh_done, 1)

            for s in range(NU):
                leading(s, 16, s, None)
            with act.Fori(0, NP_HEADS) as i:
                def copy_leading(h):
                    if h == 0:
                        act.wait_ge(pairs_done, i + 1)
                        act.wait_ge(rope_done, 12 * i + 6)
                    else:
                        act.wait_ge(rope_done, 12 * i + 12)
                        act.wait_ge(s1_mm, 8 * i + 4)
                    nc.scalar.activation(QKh[0:HEAD, 0, :, :], Qh[h][0:HEAD, :, :], ACT.Copy)
                    if h == 0:
                        act.wait_ge(rope_done, 12 * i + 10)
                        nc.scalar.activation(QKh[0:HEAD, 1, 0:2, :], Kh[h][0:HEAD, 0:2, :], ACT.Copy)
                        act.wait_ge(rope_done, 12 * i + 11)
                        nc.scalar.activation(QKh[0:HEAD, 1, 2, :], Kh[h][0:HEAD, 2, :], ACT.Copy).then_inc(hi_done, 1)
                    else:
                        nc.scalar.activation(QKh[0:HEAD, 1, :, :], Kh[h][0:HEAD, :, :], ACT.Copy).then_inc(hi_done, 1)

                for u in range(9):
                    g = u - 6
                    if g >= 0:
                        act.wait_ge(unit_mm, 9 * i + (u + 1))
                        if g > 0:
                            act.wait_ge(v_mm, 3 * i + g)
                        nc.scalar.activation(vT[:, :], PS[2 + g % 2][:, :], ACT.Copy).then_inc(vT_done, 1)
                    leading(u % NU, 48 * i + 16 * (u // NU + 2), u, 9 * i + (u + 1))
                    if u == 5:
                        copy_leading(0)
                    if u == 6:
                        copy_leading(1)
                    if g >= 0:
                        act.wait_ge(v_mm, 3 * i + (g + 1))
                        nc.scalar.activation(Vs[:, g, :, :, 0:HEAD], PS[2 + g % 2][:, :].rearrange("p (n h d) -> p n h d", n=NT, h=2),
                                             ACT.Copy).then_inc(v_done, 1)
                for h in range(2):
                    for k in range(4):
                        act.wait_ge(s2_mm, 8 * i + (4 * h + k + 1))
                        w = 384 if k == 3 else 512
                        nc.scalar.activation(Pm[h][:, k * 512:k * 512 + w], PS[4 + k][:, 0:w], ACT.Exp).then_inc(exp_done, 1)
            for c in range(KT):
                act.wait_ge(oT_done, 2 * NP_HEADS)
                nc.scalar.activation(HQh[:, c, :], oT[:, c, :], ACT.Copy).then_inc(oTh_done, 1)
                if c + NU < KT:
                    m = 9 * NP_HEADS + c + NU
                    leading(m % NU, 16 * (m // NU + 1), m, m - NU + 1)
            moe_act(1)
            norm_act("out")

        @block.vector
        def _(dve):
            steps = Steps(dve, v_steps)
            V = nc.vector
            V.memset(tick[0:1, :], 0.0).then_inc(pairs_done, 1)
            V.memset(rowt[0:1, :], 0.0).then_inc(row_done, 1)

            def norm_dve(k):
                dve.wait_ge(sq_done.sem, sq_done.at(k, NT))
                V.tensor_scalar(ss[:, :], ss[:, :], 1.0 / D, EPS, ALU.mult, ALU.add).then_inc(var_ready.sem, 1)
                dve.wait_ge(std_ready.sem, std_ready.at(k, 1))
                steps.step(V.reciprocal(rstd[:, :], rstd[:, :]))
                for n in range(NT):
                    V.tensor_scalar(XN[k][:, n, :], X[:, n, :], rstd[:, n:n + 1], None, ALU.mult).then_inc(xn_ready.sem, 1)
                if k == "out":
                    return
                if k == "kv":
                    for kt in range(KT):
                        dve.wait_ge(ht_act.sem, ht_act.at(k, 2 * kt + 2))
                        for dst, hi, v in ((HTl, HTh, V_NORM["kv"]), (HQl, HQh, V_NORM["q"])):
                            V.scalar_tensor_tensor(dst[:, kt, :], PS[kt][:, :], vn[:, v + kt:v + kt + 1], hi[:, kt, :].bitcast(F32),
                                                   ALU.mult, ALU.subtract).then_inc(ht_dve.sem, 1)
                else:
                    for kt in range(1, KT, 2):
                        dve.wait_ge(xT_ready.sem, xT_ready.at(k, kt + 1))
                        V.tensor_scalar(HT[:, kt, :], PS[kt][:, :], vn[:, V_NORM[k] + kt:V_NORM[k] + kt + 1], None, ALU.mult).then_inc(ht_dve.sem, 1)

            dve.wait_ge(const_in, 48)
            norm_dve("a")
            dve.wait_ge(cvec_in, 16)
            dve.wait_ge(conv_init, 1)
            nv = CONV - POOL_TAPS
            per = 2 * (1 + nv + 1)
            with dve.Fori(0, KT // 2) as i:
                steps.enter(i, per)
                for b in range(2):
                    steps.step(V.tensor_copy(taps_v[b][:, 0:nv], cv[:, bass.ds((2 * i + b) * CONV + C_WDW, nv)]))
                    dve.wait_ge(sig_done[b], i + 1)
                    dve.wait_ge(pool_conv[b], i)
                    V.scalar_tensor_tensor(upad[b][:, PAD:PAD + T], PS[2 * b][:, :], cv[:, bass.ds(2 * i + b + C_BIN, 1)], sig[b],
                                           ALU.add, ALU.mult).then_inc(glu_done[b], 1)
                    dve.wait_ge(glu_done[b], i + 1)
                    steps.mark(V.tensor_scalar(accv[0], upad[b][:, 0:T], taps_v[b][:, 0:1], None, ALU.mult))
                    steps.mark(V.tensor_scalar(accv[1], upad[b][:, 1:1 + T], taps_v[b][:, 1:2], cv[:, bass.ds(2 * i + b + C_BDW, 1)], ALU.mult, ALU.add))
                    for t in range(2, nv):
                        steps.wait(1)
                        steps.mark(V.scalar_tensor_tensor(accv[t % 2], upad[b][:, t:t + T], taps_v[b][:, t:t + 1], accv[t % 2], ALU.mult, ALU.add))
                    steps.wait()
                    steps.step(V.tensor_tensor(accv[0], accv[0], accv[1], ALU.add))
                    dve.wait_ge(pool_conv[b], i + 1)
                    V.tensor_tensor(HTQ[:, bass.ds(2 * i + b, 1), :].rearrange("p a b -> p (a b)"), accv[0], accp[b], ALU.add).then_inc(conv_done[b], 1)
                steps.leave(KT // 2)
            dve.wait_ge(mean_mm, 1)
            for b in range(2):
                dve.wait_ge(conv_done[b], KT // 2)
            for c in range(KT):
                V.tensor_tensor(HTQ[:, c, :], HTQ[:, c, :], PS[4][:, :], ALU.subtract).then_inc(ln_d, 1)
            dve.wait_ge(var_mm, KT)
            V.tensor_scalar(lnstd, PS[5][:, :], EPS, None, ALU.add).then_inc(lnvar_ready, 1)
            dve.wait_ge(lnstd_ready, 1)
            steps.step(V.reciprocal(lnstd, lnstd))
            dve.wait_ge(ln_d, KT)
            for c in range(KT):
                V.tensor_tensor(HTQ[:, c, :], HTQ[:, c, :], lnstd, ALU.mult).then_inc(ln_n, 1)
            dve.wait_ge(bout_added, NT)
            for n in range(NT):
                for h in range(2):
                    dve.wait_ge(wout_mm, 2 * n + h + 1)
                    ins = V.tensor_tensor(X[:, n, h * 512:(h + 1) * 512], X[:, n, h * 512:(h + 1) * 512], PS[2 * n + h][:, :], ALU.add)
                    steps.mark(ins) if h == 0 else ins.then_inc(x_upd.sem, 1)

            def bc(ap, *shape):
                return ap.to_broadcast(list(shape))

            def first_max(values, top1, onehot, scratch):
                steps.step(V.tensor_reduce(top1, values, AX, ALU.max))
                steps.step(V.tensor_tensor(onehot, values, bc(top1, P, NT, EG), ALU.is_equal))
                steps.step(V.tensor_tensor(onehot, onehot, tie_w.rearrange("p (a b) -> p a b", a=1).to_broadcast([P, NT, EG]), ALU.mult))
                steps.step(V.tensor_reduce(scratch, onehot, AX, ALU.max))
                steps.step(V.tensor_tensor(onehot, onehot, bc(scratch, P, NT, EG), ALU.is_equal))

            def routing(l):
                dve.wait_ge(xn_stored.sem, xn_stored.at(l, NT * 16))
                dve.wait_ge(xT_ready.sem, xT_ready.at(f"f{l}", KT))
                for g in range(EG):
                    steps.mark(V.memset(tie_w[:, g:g + 1], float(EG - g)))
                for e in range(E):
                    steps.mark(V.memset(eidx[:, e:e + 1], float(e)))
                    steps.mark(V.memset(pos[:, 0, e:e + 1], float(e)))
                for c in range(MAXC + 1):
                    steps.mark(V.memset(limits[:, c:c + 1], float(c * P)))
                for c in range(XB):
                    steps.mark(V.memset(xcols[:, c:c + 1], float(E + c)))
                steps.mark(V.memset(ones48, 1.0))
                dve.wait_ge(logit_mm.sem, logit_mm.at(l, 1))
                steps.step(V.tensor_copy(lg, PS[0][:, 0:NT * (EG + E)].rearrange("p (n e) -> p n e", n=NT)))
                lgrp, lexp = lg[:, :, 0:EG], lg[:, :, EG:EG + E]
                first_max(lgrp, gmax, gsel, gsum)
                V_g = V.tensor_tensor(gexp, lgrp, bc(gmax, P, NT, EG), ALU.subtract)
                steps.step(V_g)
                l4 = lexp.rearrange("p n (g e) -> p n e g", g=EG)
                steps.step(V.tensor_tensor(prod, l4, gsel[:, :, :].rearrange("p n (o g) -> p n o g", o=1).to_broadcast([P, NT, EG, EG]), ALU.mult))
                steps.step(V.tensor_reduce(sel[:, :, :].rearrange("p n (e o) -> p n e o", o=1), prod, AX, ALU.add))
                first_max(sel, top[0], esel[0], pick)
                steps.step(V.tensor_scalar(tmp4, esel[0], -3e38, None, ALU.mult))
                steps.step(V.tensor_tensor(tmp4, tmp4, sel, ALU.add))
                first_max(tmp4, top[1], esel[1], pick)
                V.tensor_tensor(pick, top[1], top[0], ALU.subtract).then_inc(gdiff.sem, 1)
                for k in range(2):
                    steps.mark(V.tensor_tensor(hot[k], gsel[:, :, :].rearrange("p n (g o) -> p n g o", o=1).to_broadcast([P, NT, EG, EG]),
                                               esel[k].rearrange("p n (o e) -> p n o e", o=1).to_broadcast([P, NT, EG, EG]), ALU.mult))
                steps.wait()
                hotf = [hot[k].rearrange("p n g e -> p n (g e)") for k in range(2)]
                V.tensor_tensor(both, hotf[0], hotf[1], ALU.add).then_inc(both_ready.sem, 1)
                dve.wait_ge(gexp_done.sem, gexp_done.at(l, 2))
                steps.mark(V.tensor_reduce(gsum, gexp, AX, ALU.add))
                steps.step(V.tensor_scalar(top[0], pick, 1.0, None, ALU.add))
                steps.step(V.tensor_tensor(gsum, gsum, top[0], ALU.mult))
                steps.step(V.reciprocal(wt[0], gsum))
                steps.step(V.tensor_tensor(wt[1], wt[0], pick, ALU.mult))
                dve.wait_ge(rank_mm.sem, rank_mm.at(l, 1))
                steps.mark(V.tensor_copy(rank, PS[1][:, 0:NT * E].rearrange("p (n e) -> p n e", n=NT)))
                steps.step(V.tensor_copy(count, PS[1][:, NT * E:NT * E + E]))
                flat = "p a b -> p (a b)"

                def spread(ap, pat, *shape, **kw):
                    return ap.rearrange(pat, **kw).to_broadcast(list(shape))

                for c in range(1, MAXC):
                    steps.mark(V.tensor_scalar(over[:, c - 1, :], count, float(c * P), None, ALU.is_gt))
                steps.wait()
                steps.step(V.tensor_tensor_scan(pos[:, 1:, :].rearrange(flat), ones48.rearrange(flat), over.rearrange(flat), float(E - 1), ALU.mult, ALU.add))
                steps.mark(V.tensor_scalar(nover, pos[:, MAXC - 1, E - 1:E], float(E - 1), None, ALU.subtract))
                steps.step(V.tensor_tensor(match.rearrange("p x c e -> p x (c e)"), spread(pos[:, 1:, :], "p (o c) e -> p o (c e)", P, XB, (MAXC - 1) * E, o=1),
                                           spread(xcols, "p (x o) -> p x o", P, XB, (MAXC - 1) * E, o=1), ALU.is_equal))
                steps.step(V.tensor_tensor(match.rearrange("p x c e -> p x (c e)"), match.rearrange("p x c e -> p x (c e)"),
                                           spread(over, "p (o c) e -> p o (c e)", P, XB, (MAXC - 1) * E, o=1), ALU.mult))
                steps.step(V.tensor_tensor(match.rearrange("p x c e -> p (x c) e"), match.rearrange("p x c e -> p (x c) e"),
                                           spread(eidx, "p (o e) -> p o e", P, XB * (MAXC - 1), E, o=1), ALU.mult))
                steps.step(V.tensor_reduce(blk_f, match.rearrange("p x c e -> p x (c e)"), AX, ALU.add))
                steps.mark(V.tensor_copy(blk_e[:, 0:E], eidx))
                steps.mark(V.tensor_copy(blk_e[:, E:E + XB], blk_f))
                for q in range(4):
                    steps.mark(V.tensor_scalar(half4[:, q:q + 1], nover, float(2 * q), None, ALU.is_gt))
                steps.wait()
                steps.step(V.tensor_reduce(nover, half4, AX, ALU.add))
                steps.mark(V.tensor_scalar(npair_i, nover, float(E // 2), None, ALU.add))
                steps.step(V.tensor_tensor(hr[:, 0:NT, :], hotf[0], rank, ALU.mult))
                steps.step(V.tensor_tensor(hr[:, NT:2 * NT, :], hotf[1], rank, ALU.mult))
                steps.step(V.tensor_reduce(rk, hr, AX, ALU.add))
                steps.step(V.tensor_tensor(ge, spread(rk, "p (k o) -> p k o", P, 2 * NT, MAXC + 1, o=1), spread(limits, "p (o c) -> p o c", P, 2 * NT, MAXC + 1, o=1), ALU.is_ge))
                steps.mark(V.tensor_tensor(inblk, ge[:, :, 0:MAXC], ge[:, :, 1:MAXC + 1], ALU.subtract))
                steps.step(V.tensor_reduce(gadd, ge[:, :, 1:MAXC], AX, ALU.add))
                steps.mark(V.scalar_tensor_tensor(rk, gadd, float(-P), rk, ALU.mult, ALU.add))
                for k in range(2):
                    steps.mark(V.tensor_tensor(big[:, k * NT:(k + 1) * NT, :, :], spread(hotf[k], "p n (o e) -> p n o e", P, NT, MAXC, E, o=1),
                                               spread(pos, "p (o c) e -> p o c e", P, NT, MAXC, E, o=1), ALU.mult))
                steps.wait()
                steps.step(V.tensor_reduce(col4, big, AX, ALU.add))
                steps.step(V.tensor_tensor(col4, col4, inblk, ALU.mult))
                steps.step(V.tensor_reduce(col, col4, AX, ALU.add))
                V.scalar_tensor_tensor(slot_addr, rk, float(SLOTS), col, ALU.mult, ALU.add).then_inc(routed.sem, 1)
                dve.wait_ge(slots_in.sem, slots_in.at(l, 16))
                steps.step(V.tensor_scalar(src_f, slot_ids, float(T), float(-T), ALU.is_ge, ALU.mult))
                V.tensor_tensor(src_ids, src_f, slot_ids, ALU.add).then_inc(src_ready.sem, 1)

            def moe_dve(l, after):
                norm_dve(f"f{l}")
                routing(l)
                npair = dve.value_load(npair_i[0:1, 0:1], min_val=E // 2, max_val=(E + XB) // 2)
                gain = vn[:, V_NORM[f"f{l}"]:V_NORM[f"f{l}"] + KT]

                def copy_xgT(b, n):
                    dve.wait_ge(xgT_mm[l][b], n)
                    for q in range(2):
                        ins = V.tensor_tensor(xgT[b][:, 4 * q:4 * q + 4, :], PS[5 + q][:, :].rearrange("p (a b) -> p a b", a=4),
                                              gain[:, 4 * q:4 * q + 4].rearrange("p (a o) -> p a o", o=1).to_broadcast([P, 4, P]), ALU.mult)
                    ins.then_inc(xgT_done[l][b], 1)

                for b in range(2):
                    copy_xgT(b, 1)
                with dve.Fori(0, npair) as i:
                    def hidden(b):
                        dve.wait_ge(sil_done[l], 2 * i + b + 1)
                        dve.wait_ge(up_mm[l], 2 * i + b + 1)
                        dve.wait_ge(hT_mm[l], 2 * i + b)
                        V.tensor_tensor(hid, PS[1][:, :], sil, ALU.mult).then_inc(hid_done[l], 1)

                    def copy_hidT(b):
                        dve.wait_ge(hT_mm[l], 2 * i + b + 1)
                        dve.wait_ge(down_mm[l], 2 * i + b)
                        V.tensor_copy(hidT.rearrange("p a b -> p (a b)"), PS[2][:, :]).then_inc(hidT_done[l], 1)

                    for b in range(2):
                        hidden(b)
                        copy_hidT(b)
                        copy_xgT(b, i + 2)
                V.tensor_copy(nover, half4[:, 0:1]).then_inc(xg_idle.sem, 1)
                for n in range(NT):
                    dve.wait_ge(y_back[n], 32 * (l + 1))
                    steps.step(V.scalar_tensor_tensor(X[:, n, :], yg[0][:, n, :], wt[0][:, n, :], X[:, n, :], ALU.mult, ALU.add))
                    V.scalar_tensor_tensor(X[:, n, :], yg[1][:, n, :], wt[1][:, n, :], X[:, n, :], ALU.mult, ALU.add).then_inc(x_upd.sem, 1)

            moe_dve(0, "kv")
            dve.wait_ge(x_upd.sem, x_upd.at("kv", NT))
            norm_dve("kv")
            dve.wait_ge(att_const, 32)

            def trailing(s, m):
                dve.wait_ge(wh_done, m)
                V.tensor_tensor(wl[:, s, :], wraw[:, s, :], wh[:, s, :].bitcast(F32), ALU.subtract).then_inc(wl_done, 1)

            for s in range(NU):
                trailing(s, s + 1)
            per = 2 * 5 + 2 * 1 + 2 * 1
            with dve.Fori(0, NP_HEADS) as i:
                steps.enter(i, per)
                for t in range(6):
                    tab = 2 if t < 3 else 0
                    src = PS[t % 2]
                    dve.wait_ge(unit_mm, 9 * i + (t + 1))
                    if t < 2:
                        dve.wait_ge(pairs_done, i + 1)
                    else:
                        dve.wait_ge(rope_done, 12 * i + 2 * (t - 1))
                    V.tensor_tensor(rope_ab[:, 2 * (t % 2), :], src[:, :], rope_t[:, tab, :], ALU.mult)
                    for q in range(4):
                        s, d = 32 * (q ^ 1), 32 * q
                        ins = V.tensor_tensor(rope_ab[d:d + 32, 2 * (t % 2) + 1, :], src[s:s + 32, :], rope_t[s:s + 32, tab + 1, :], ALU.mult)
                    ins.then_inc(rope_ab_done, 1)
                    trailing(t % NU, 9 * i + (t + NU + 1))
                trailing(0, 9 * i + (6 + NU + 1))

                def maxima(h):
                    dve.wait_ge(s1_mm, 8 * i + (4 * h + 1))
                    steps.mark(V.tensor_reduce(NM[:, 1:3], PS[4][:, :].rearrange("p (a b) -> p a b", a=2), AX, ALU.max, negate=True))
                    dve.wait_ge(s1_mm, 8 * i + (4 * h + 2))
                    steps.mark(V.tensor_reduce(NM[:, 0:1], PS[5][:, 0:P], AX, ALU.max, negate=True))
                    steps.mark(V.tensor_reduce(NM[:, 3:4], PS[5][:, P:3 * P], AX, ALU.max, negate=True))
                    for k in (2, 3):
                        dve.wait_ge(s1_mm, 8 * i + (4 * h + k + 1))
                        steps.mark(V.tensor_reduce(NM[:, 4 * k - 4:4 * k], PS[4 + k][:, :].rearrange("p (a b) -> p a b", a=4), AX, ALU.max, negate=True))
                    steps.wait()
                    V.tensor_tensor(NM[:, 4:8], NM[:, 4:8], NM[:, 8:12], ALU.min).then_inc(max_done, 1)

                def maxima_row(h):
                    dve.wait_ge(row_mm, 2 * i + (h + 1))
                    steps.step(V.tensor_copy(rowt[0:1, :], PS[0][0:1, :]))
                    one = "p (o t) -> p o t"
                    V.tensor_tensor(Qh[h][HEAD:HEAD + 1, :, :], PS[1][0:1, :].rearrange(one, o=1).to_broadcast([1, NG, T]),
                                    rowt[0:1, :].rearrange(one, o=1).to_broadcast([1, NG, T]), ALU.min).then_inc(row_done, 1)

                maxima(0)
                maxima_row(0)
                maxima(1)
                trailing(1, 9 * i + (7 + NU + 1))
                maxima_row(1)
                trailing(2, 9 * i + (8 + NU + 1))
                for h in range(2):
                    O = PS[3 - h]
                    dve.wait_ge(pv_mm, 2 * i + (h + 1))
                    inv = rope_ab[0:HEAD, h, :]
                    steps.step(V.reciprocal(inv, O[HEAD:P, :]))
                    V.tensor_tensor(oT[h * HEAD:(h + 1) * HEAD, bass.ds(i, 1), :].rearrange("p a b -> p (a b)"), O[0:HEAD, :], inv, ALU.mult).then_inc(oT_done, 1)
                dve.wait_ge(oT_done, 2 * i + 2)
                V.tensor_copy(tick[0:1, :], vn[0:1, 0:1]).then_inc(pairs_done, 1)
                steps.leave(NP_HEADS)
            for c in range(KT):
                dve.wait_ge(oTh_done, c + 1)
                V.tensor_tensor(HQl[:, c, :], oT[:, c, :], HQh[:, c, :].bitcast(F32), ALU.subtract).then_inc(oTl_done, 1)
                if c + NU < KT:
                    trailing(c % NU, 9 * NP_HEADS + c + NU + 1)
            for n in range(NT):
                for h in range(2):
                    dve.wait_ge(wo_mm, 2 * n + h + 1)
                    ins = V.tensor_tensor(X[:, n, h * 512:(h + 1) * 512], X[:, n, h * 512:(h + 1) * 512], PS[2 * n + h][:, :], ALU.add)
                    steps.mark(ins) if h == 0 else ins.then_inc(x_upd.sem, 1)
            moe_dve(1, "out")
            dve.wait_ge(x_upd.sem, x_upd.at("out", NT))
            norm_dve("out")
            dve.wait_ge(fin_in, 16)
            dve.wait_ge(xn_ready.sem, xn_ready.at("out", NT))
            for n in range(NT):
                V.tensor_tensor(XN["out"][:, n, :], XN["out"][:, n, :], fin_g, ALU.mult).then_inc(y_ready, 1)

        @block.tensor
        def _(pe):
            M = nc.tensor

            def norm_pe(k):
                for n in range(NT):
                    pe.wait_ge(xn_ready.sem, xn_ready.at(k, n + 1))
                    for kt in range(KT):
                        ins = M.transpose(PS[kt][:, n * P:(n + 1) * P], XN[k][:, n, kt::KT], ident[:, :])
                        if n == NT - 1:
                            ins.then_inc(xT_ready.sem, 1)

            def normed(k):
                n = 2 * KT if k == "kv" else KT // 2
                pe.wait_ge(ht_act.sem, ht_act.at(k, n))
                pe.wait_ge(ht_dve.sem, ht_dve.at(k, n))

            pe.wait_ge(const_in, 48)
            norm_pe("a")
            normed("a")
            with pe.Fori(0, KT // 2) as i:
                for b in range(2):
                    pe.wait_ge(win_in[b], (i + 1) * 16)
                    pe.wait_ge(glu_done[b], i)
                    for s in range(2):
                        for kt in range(KT):
                            ins = M.matmul(PS[2 * b + s][:, :], w_in_sb[b][:, kt, s, :], HT[:, kt, :], start=kt == 0, stop=kt == KT - 1)
                    ins.then_inc(u_mm[b], 1)
            pe.wait_ge(conv_init, 1)
            for b in range(2):
                pe.wait_ge(conv_done[b], KT // 2)
            for c in range(KT):
                ins = M.matmul(PS[4][:, :], onesf, HTQ[:, c, :], start=c == 0, stop=c == KT - 1)
            ins.then_inc(mean_mm, 1)
            for c in range(KT):
                pe.wait_ge(ln_sq, c + 1)
                M.matmul(PS[5][:, :], onesf, lnsq[c % 2], start=c == 0, stop=c == KT - 1).then_inc(var_mm, 1)
            pe.wait_ge(wout_in, 16)
            pe.wait_ge(lnvar_ready, 1)
            for c in range(KT):
                pe.wait_ge(silu_done, c + 1)
                for n in range(NT):
                    for h in range(2):
                        ins = M.matmul(PS[2 * n + h][:, :], HTQ[:, c, n * P:(n + 1) * P], WO[:, c, h * 512:(h + 1) * 512],
                                       start=c == 0, stop=c == KT - 1)
                        if c == KT - 1:
                            ins.then_inc(wout_mm, 1)

            def moe_pe(l):
                norm_pe(f"f{l}")
                normed(f"f{l}")
                pe.wait_ge(rt_in.sem, rt_in.at(l, 16))
                for n in range(NT):
                    for kt in range(KT):
                        ins = M.matmul(PS[0][:, n * (EG + E):(n + 1) * (EG + E)], HT[:, kt, n * P:(n + 1) * P], rt[:, kt, :],
                                       start=kt == 0, stop=kt == KT - 1)
                ins.then_inc(logit_mm.sem, 1)
                pe.wait_ge(both_ready.sem, both_ready.at(l, 1))
                for n in range(NT + 1):
                    for m in range(min(n + 1, NT)):
                        ins = M.matmul(PS[1][:, n * E:(n + 1) * E], before_b if m == n else ones_b, both[:, m, :],
                                       start=m == 0, stop=m == min(n, NT - 1))
                ins.then_inc(rank_mm.sem, 1)
                pe.wait_ge(routed.sem, routed.at(l, 1))
                npair = pe.value_load(npair_i[0:1, 0:1], min_val=E // 2, max_val=(E + XB) // 2)

                def transpose_rows(b, n):
                    pe.wait_ge(gathered[l][b], n * 16)
                    pe.wait_ge(xgT_done[l][1 - b], n - 1 if b == 0 else n)
                    for kt in range(KT):
                        ins = M.transpose(PS[5 + kt // 4][:, (kt % 4) * P:(kt % 4 + 1) * P], xg[b][:, kt::KT], ident[:, :])
                    ins.then_inc(xgT_mm[l][b], 1)

                for b in range(2):
                    transpose_rows(b, 1)
                with pe.Fori(0, npair) as i:
                    def gate(b):
                        pe.wait_ge(wg_in[l][b], (i + 1) * 16)
                        pe.wait_ge(xgT_done[l][b], i + 1)
                        pe.wait_ge(sil_done[l], 2 * i + b)
                        for kt in range(KT):
                            ins = M.matmul(PS[0][:, :], xgT[b][:, kt, :], wg[b][:, kt, :], start=kt == 0, stop=kt == KT - 1)
                        ins.then_inc(gate_mm[l], 1)

                    def up(b):
                        pe.wait_ge(wu_in[l][b], (i + 1) * 16)
                        pe.wait_ge(hid_done[l], 2 * i + b)
                        for kt in range(KT):
                            ins = M.matmul(PS[1][:, :], xgT[b][:, kt, :], wu[b][:, kt, :], start=kt == 0, stop=kt == KT - 1)
                        ins.then_inc(up_mm[l], 1)

                    def transpose_hidden(b):
                        pe.wait_ge(hid_done[l], 2 * i + b + 1)
                        pe.wait_ge(hidT_done[l], 2 * i + b)
                        for ft in range(FT):
                            ins = M.transpose(PS[2][:, ft * P:(ft + 1) * P], hid[:, ft::FT], ident[:, :])
                        ins.then_inc(hT_mm[l], 1)

                    def down(b):
                        pe.wait_ge(wd_in[l][b], (i + 1) * 16)
                        pe.wait_ge(hidT_done[l], 2 * i + b + 1)
                        pe.wait_ge(y_done[l], 2 * i + b)
                        for h in range(2):
                            for ft in range(FT):
                                ins = M.matmul(PS[3 + h][:, :], hidT[:, ft, :], wd[b][:, ft, h * 512:(h + 1) * 512],
                                               start=ft == 0, stop=ft == FT - 1)
                        ins.then_inc(down_mm[l], 1)

                    gate(0)
                    up(0)
                    gate(1)
                    transpose_hidden(0)
                    transpose_rows(0, i + 2)
                    up(1)
                    down(0)
                    transpose_hidden(1)
                    transpose_rows(1, i + 2)
                    down(1)

            moe_pe(0)
            norm_pe("kv")
            normed("kv")
            pe.wait_ge(att_const, 32)
            pe.wait_ge(att_init, 1)

            with pe.Fori(0, NP_HEADS) as i:
                def tile_of(g, n):
                    return slice(n * P, (n + 1) * P) if g == 0 else slice(n, T, NT)

                for t in range(6):
                    hi, lo, g = (HQh, HQl, t) if t < 3 else (HTh, HTl, t - 3)
                    pe.wait_ge(wl_done, 9 * i + (t + 1))
                    if t < 2:
                        pe.wait_ge(row_done, 2 * i + 1)
                    else:
                        pe.wait_ge(rope_ab_done, 6 * i + (t - 1))
                    for kt in range(KT):
                        whk, wlk = wh[:, t % NU, kt * P:(kt + 1) * P], wl[:, t % NU, kt * P:(kt + 1) * P]
                        M.matmul(PS[t % 2][:, :], whk, hi[:, kt, :], start=kt == 0, stop=False)
                        M.matmul(PS[t % 2][:, :], whk, lo[:, kt, :], start=False, stop=False)
                        ins = M.matmul(PS[t % 2][:, :], wlk, hi[:, kt, :], start=False, stop=kt == KT - 1)
                    ins.then_inc(unit_mm, 1)

                def values(g):
                    pe.wait_ge(wl_done, 9 * i + (7 + g))
                    if g == 0:
                        pe.wait_ge(pairs_done, i + 1)
                    if g == 2:
                        pe.wait_ge(v_done, 3 * i + 1)
                    dst = PS[2 + g % 2][:, :]
                    for kt in range(KT):
                        whk, wlk = wh[:, g, kt * P:(kt + 1) * P], wl[:, g, kt * P:(kt + 1) * P]
                        M.matmul(dst, whk, HTh[:, kt, :], start=kt == 0, stop=False)
                        M.matmul(dst, whk, HTl[:, kt, :], start=False, stop=False)
                        ins = M.matmul(dst, wlk, HTh[:, kt, :], start=False, stop=kt == KT - 1)
                    ins.then_inc(unit_mm, 1)

                def turn(g):
                    pe.wait_ge(vT_done, 3 * i + (g + 1))
                    for n in range(NT):
                        ins = M.transpose(PS[2 + g % 2][:, n * P:(n + 1) * P], vT[:, tile_of(g, n)], ident[:, :])
                    ins.then_inc(v_mm, 1)

                def lay_mask(bank, blocks):
                    if len(set(blocks)) == 1:
                        M.matmul(PS[bank][:, :], ident_b, masks_b[:, blocks[0]:blocks[0] + 1, :].to_broadcast([P, 4, P]), start=True, stop=False)
                    else:
                        for j, m in enumerate(blocks):
                            M.matmul(PS[bank][:, j * P:(j + 1) * P], ident_b, masks_b[:, m, :], start=j == 0, stop=False)

                def scores(h):
                    if h == 0:
                        pe.wait_ge(pairs_done, i + 1)
                    else:
                        pe.wait_ge(max_done, 2 * i + 1)
                    pe.wait_ge(hi_done, 2 * i + (h + 1))
                    q, k = QKh[:, 0, :, :], QKh[:, 1, :, :]
                    for s, (mask, parts) in enumerate((
                            ([PREV, OWN, PREV, OWN], [(0, 1, 0, 256), (0, 2, 256, 256)]),
                            ([OWN, PREV, OWN], [(0, 0, 0, 128), (0, 3, 128, 256)]),
                            ([OWN] * 4, [(1, n, n * P, 128) for n in range(NT)]),
                            ([PHASE] * 4, [(2, n, n * P, 128) for n in range(NT)]))):
                        lay_mask(4 + s, mask)
                        for j, (g, n, at, w) in enumerate(parts):
                            keys = slice((n + 1) * P - w, (n + 1) * P) if g == 0 else tile_of(g, n)
                            ins = M.matmul(PS[4 + s][:, at:at + w], q[0:HEAD, g, tile_of(g, n)], k[0:HEAD, g, keys],
                                           start=False, stop=j == len(parts) - 1)
                        ins.then_inc(s1_mm, 1)

                def max_rows(h):
                    pe.wait_ge(max_done, 2 * i + (h + 1))
                    if h == 1:
                        pe.wait_ge(row_done, 2 * i + 2)
                    for n in range(NT):
                        M.transpose(PS[0][0:1, n * P:(n + 1) * P], NM[:, n:n + 1], ident[:, :])
                    for n in range(NT):
                        ins = M.transpose(PS[1][0:1, n::NT], NM[:, NT + n:NT + n + 1], ident[:, :])
                    ins.then_inc(row_mm, 1)

                def scores_t(h):
                    pe.wait_ge(row_done, 2 * i + (h + 2))
                    q, k = Qh[h], Kh[h]
                    for s, (mask, parts) in enumerate((
                            ([OWN_T] * 4, [(1, n, n * P, 128) for n in range(NT)]),
                            ([PHASE_T] * 4, [(2, n, n * P, 128) for n in range(NT)]),
                            ([OWN_T, PREV_T, OWN_T, PREV_T], [(0, 0, 0, 256), (0, 1, 256, 256)]),
                            ([OWN_T, PREV_T, OWN_T], [(0, 2, 0, 256), (0, 3, 256, 128)]))):
                        if h == 0:
                            pe.wait_ge(max_done, 2 * i + 2)
                        else:
                            pe.wait_ge(exp_done, 8 * i + (s + 1))
                        lay_mask(4 + s, mask)
                        for j, (g, n, at, w) in enumerate(parts):
                            queries = slice(n * P, n * P + w) if g == 0 else tile_of(g, n)
                            ins = M.matmul(PS[4 + s][:, at:at + w], k[0:HEAD + 1, g, tile_of(g, n)], q[0:HEAD + 1, g, queries],
                                           start=False, stop=j == len(parts) - 1)
                        ins.then_inc(s2_mm, 1)

                def weigh(h):
                    pe.wait_ge(v_done, 3 * i + 3)
                    O = PS[3 - h]
                    for s, parts in enumerate((
                            [(1, n, n * P, 128) for n in range(NT)],
                            [(2, n, n * P, 128) for n in range(NT)],
                            [(0, 0, 0, 256), (0, 1, 256, 256)],
                            [(0, 2, 0, 256), (0, 3, 256, 128)])):
                        pe.wait_ge(exp_done, 8 * i + (4 * h + s + 1))
                        for g, n, at, w in parts:
                            queries = slice(n * P, n * P + w) if g == 0 else tile_of(g, n)
                            ins = M.matmul(O[:, queries], Vs[:, g, n, h, :], Pm[h][:, s * 512 + at:s * 512 + at + w],
                                           start=s == 0 and n == 0, stop=s == 3 and n == 3)
                    ins.then_inc(pv_mm, 1)

                values(0)
                scores(0)
                turn(0)
                values(1)
                max_rows(0)
                scores(1)
                turn(1)
                values(2)
                max_rows(1)
                turn(2)
                scores_t(0)
                scores_t(1)
                weigh(0)
                weigh(1)
            pe.wait_ge(pairs_done, NP_HEADS + 1)
            for c in range(KT):
                u = (9 * NP_HEADS + c) % NU
                pe.wait_ge(wl_done, 9 * NP_HEADS + c + 1)
                pe.wait_ge(oTl_done, c + 1)
                for n in range(NT):
                    tok_n = slice(n * P, (n + 1) * P)
                    for h in range(2):
                        cols = slice(h * 512, (h + 1) * 512)
                        dst = PS[2 * n + h][:, :]
                        M.matmul(dst, HQh[:, c, tok_n], wh[:, u, cols], start=c == 0, stop=False)
                        M.matmul(dst, HQh[:, c, tok_n], wl[:, u, cols], start=False, stop=False)
                        ins = M.matmul(dst, HQl[:, c, tok_n], wh[:, u, cols], start=False, stop=c == KT - 1)
                        if c == KT - 1:
                            ins.then_inc(wo_mm, 1)
                if c < KT - 1:
                    ins.then_inc(unit_mm, 1)
            moe_pe(1)


def bf16_bits(x):
    import numpy as np
    return (np.ascontiguousarray(x, np.float32).view(np.uint32) >> 16).astype(np.uint16)


def constants():
    import numpy as np
    i, j = np.arange(P)[:, None], np.arange(P)[None, :]
    ident = np.eye(P, dtype=np.float32)
    c16 = bf16_bits(np.concatenate([ident, (i < j).astype(np.float32), np.ones((P, P), np.float32)], 1))
    no = np.float32(-BIG)
    own = np.where(j <= i, np.float32(0), no)
    prev = np.where(j >= i, np.float32(0), no)
    phase = np.where((i - j) % 4 == 0, own, no)
    masks = bf16_bits(np.concatenate([prev, own, phase, own.T, prev.T, phase.T], 1))
    pos = np.arange(T, dtype=np.float32)
    inv = np.float32(10000.0) ** (-np.arange(0, HEAD, 2, dtype=np.float32) / np.float32(HEAD))
    ang = (inv[:, None] * pos[None, :]).astype(np.float32)
    cos = np.tile(np.cos(ang), (4, 1)).astype(np.float32)
    sin = np.tile(np.sin(ang), (4, 1)).astype(np.float32)
    sign = np.where((np.arange(P) // 32) % 2 == 0, np.float32(1), np.float32(-1))[:, None]
    scale = np.float32(HEAD ** -0.5)
    rope = np.stack([cos, sin * sign, cos * scale, sin * sign * scale], 1)
    return {"ident": ident, "c16": c16, "masks": masks, "rope": np.ascontiguousarray(rope, np.float32)}


def lay_out(i):
    import numpy as np
    f = {k: np.asarray(v) for k, v in i.items()}
    cat, asc = np.concatenate, np.ascontiguousarray
    by_row = lambda v: v.reshape(P, KT)
    by_tile = lambda v: v.reshape(-1, P).T
    a = {"x": f["x"]}
    a["norm_vecs"] = asc(cat([by_row(f["a_norm"][0]), by_row(f["ffn_norm"][0]), by_row(f["kv_norm"]),
                              by_row(f["b_norm"][0]), by_row(f["ffn_norm"][1])], 1))
    a["conv_vecs"] = asc(cat([by_tile(f["a_b_in"][0]), by_tile(f["a_b_dw"][0]), by_tile(f["a_ln_g"][0]), by_tile(f["a_ln_b"][0]),
                              f["a_w_dw"][0].reshape(CONV, KT, P).transpose(2, 1, 0).reshape(P, KT * CONV)], 1))
    a["w_in"] = asc(f["a_w_in"][0].reshape(P, KT, 2, KT, P).transpose(3, 0, 1, 2, 4).reshape(KT, P, KT * 2 * P))
    a["w_out"] = f["a_w_out"][0].reshape(KT, P, D)
    a["b_out"] = f["a_b_out"][0].reshape(1, D)
    kv = f["w_kv"].reshape(P, KT, 2, NG, NP_HEADS, P)
    q = f["b_w_q"][0].reshape(P, KT, NG, NP_HEADS, P)
    a["w_qkv"] = asc(np.stack([q, kv[:, :, 0], kv[:, :, 1]]).transpose(4, 0, 3, 1, 2, 5).reshape(NP_HEADS * 9, P, KT * P))
    a["w_o"] = f["b_w_o"][0].reshape(KT, P, D)
    a["router"] = asc(cat([f["router_group"], f["router_expert"].transpose(0, 2, 1, 3).reshape(2, D, E)], 2)
                      .reshape(2, P, KT * (EG + E)))
    for k in ("w_gate", "w_up", "w_down"):
        a[k] = f[k].reshape(2 * E, P, -1)
    a["final_norm"] = f["final_norm"].reshape(1, D)
    return a


def kernel(**inputs):
    import concourse.bacc as bacc
    from concourse.bass_utils import run_bass_kernel_spmd

    nc = bacc.Bacc("TRN2", target_bir_lowering=False, num_devices=1)
    arrays = {**lay_out(inputs), **constants()}
    aps = {n: nc.dram_tensor(n, v.shape, mybir.dt.from_np(v.dtype), kind="ExternalInput").ap() for n, v in arrays.items()}
    aps["w_out"] = aps["w_out"].rearrange("c p n -> p c n")
    aps["out"] = nc.dram_tensor("out", (1, T, D), F32, kind="ExternalOutput").ap()
    build_program(nc, aps)
    r = run_bass_kernel_spmd(nc, [arrays], core_ids=[0])
    return r.results[0]["out"]
```

```python
from contextlib import ExitStack

import concourse.bass as bass
from concourse import mybir

ALU = mybir.AluOpType
ACT = mybir.ActivationFunctionType
AX = mybir.AxisListType.X
F32 = mybir.dt.float32
F32R = mybir.dt.float32r
BF16 = mybir.dt.bfloat16
U16 = mybir.dt.uint16
U32 = mybir.dt.uint32
I32 = mybir.dt.int32

P = 128
D = 1024
T = 512
NT = T // P
KT = D // P
CONV = 31
PAD = CONV - 1
HEAD = 64
NP_HEADS = D // HEAD // 2
NG = 3
E = 16
EG = 4
F = 512
FT = F // P
EPS = 1e-6
MAXC = T // P
XB = 8
SLOTS = E + XB
NOWHERE = 8 * T
BIG = 1e30
NU = 3
POOL_TAPS = 11
GLU_AT = 8
NPROD = 4

KV_ORDER = ([(1, 0), (1, 1), (1, 2), (0, 0), (1, 3), (0, 1)] + [(1, kt) for kt in range(4, KT)]
            + [(0, kt) for kt in range(2, KT)])
Q_READY = KV_ORDER.index((1, KT - 1)) + 1

V_NORM = {"a": 0, "f0": 8, "kv": 16, "q": 24, "f1": 32}
NORM_COLS = 40
PREV, OWN, PHASE, OWN_T, PREV_T, PHASE_T = range(6)
C_BIN, C_BDW, C_LNG, C_LNB, C_WDW = 0, 16, 24, 32, 40
CONV_COLS = C_WDW + KT * CONV


class Steps:

    def __init__(self, eng, sem):
        self.eng, self.sem, self.n, self.base = eng, sem, 0, 0

    def mark(self, ins):
        ins.then_inc(self.sem, 1)
        self.n += 1

    def wait(self, back=0):
        self.eng.wait_ge(self.sem, self.base + self.n - back)

    def step(self, ins):
        self.mark(ins)
        self.wait()

    def enter(self, i, per):
        self.base = i * per + 0
        self.saved, self.per = self.n, per

    def leave(self, trips):
        assert self.n - self.saved == self.per, (self.n - self.saved, self.per)
        self.base = 0
        self.n = self.saved + self.per * trips


class Count:

    def __init__(self, sem, keys, per):
        self.sem = sem
        self.before = {k: sum(per[:i]) for i, k in enumerate(keys)}

    def at(self, key, n):
        return self.before[key] + n


def build_program(nc, a):
    x, out = a["x"], a["out"]
    xn_dram = [nc.dram_tensor(f"xn_dram{l}", (T, D), F32).ap() for l in range(2)]
    y_dram = [nc.dram_tensor(f"y_dram{l}", (2 * T, D), F32).ap() for l in range(2)]

    with ExitStack() as ctx:
        def sb(name, shape, dt=F32):
            return ctx.enter_context(nc.sbuf_tensor(name, shape, dt))

        def sem(name):
            return ctx.enter_context(nc.semaphore(name))

        base = (nc.sbuf_base + 63) // 64 * 64

        def at(name, kib, shape, dt=F32):
            return nc.alloc_sbuf_tensor_at(name, shape, dt, offset=base + int(kib * 1024))

        X = at("X", 0, [P, NT, D])
        HT = at("HT", 16, [P, KT, T])
        HTQ = at("HTQ", 32, [P, KT, T])
        WR = at("WR", 48, [P, 6 * 4096])
        WO = at("WO", 144, [P, KT, D])
        SC = at("SC", 176, [P, 7680])
        ident = at("ident_sb", 206, [P, P])
        c16 = at("c16_sb", 206.5, [P, 3 * P], U16)
        vn = at("vn", 207.25, [P, NORM_COLS])
        ss = at("ss", 207.5, [P, NT])
        rstd = at("rstd", 207.53125, [P, NT])
        idle = at("idle", 207.5625, [P, 1])
        tick = at("tick", 207.59375, [P, 1])
        spare = at("spare", 207.625, [P, 16])
        wgh, wuh = at("wgh", 16, [P, KT, F], F32R), at("wuh", 144, [P, KT, F], F32R)
        wgl = [at(f"wgl{b}", 48 + 16 * b, [P, KT, F], F32R) for b in range(2)]
        wul = [at(f"wul{b}", 80 + 16 * b, [P, KT, F], F32R) for b in range(2)]
        xgh = [at(f"xgh{b}", 160 + 4 * b, [P, KT, P], F32R) for b in range(2)]
        xgl = [at(f"xgl{b}", 168 + 4 * b, [P, KT, P], F32R) for b in range(2)]
        WOh, WOl = at("WOh", 112, [P, KT, D], F32R), at("WOl", 144, [P, KT, D], F32R)
        HTh, HTl = at("HTh", 16, [P, KT, T], F32R), at("HTl", 32, [P, KT, T], F32R)
        HQh, HQl = at("HQh", 48, [P, KT, T], F32R), at("HQl", 64, [P, KT, T], F32R)
        wraw = at("wraw", 80, [P, NU, KT * P])
        wh, wl = at("wh", 92, [P, NU, KT * P], F32R), at("wl", 104, [P, NU, KT * P], F32R)
        oT = at("oT", 116, [P, KT, T])
        KQ = at("KQ", 132, [P, 4, NG, T])
        Vs = at("Vs", 156, [P, NG, NT, 2, P])
        rope_ab = at("rope_ab", 168, [P, 4, T])
        Pm2 = at("Pm", 176, [P, 3840])
        QKh = at("QKh", 176, [P, 2, NG, T], F32R)
        masks = at("masks_sb", 191, [P, 6, P], U16)
        rope_t = at("rope_sb", 192.5, [P, 4, T])
        rowt = at("rowt", 200.5, [P, T])
        NM = at("NM", 202.5, [P, 16])
        vT = at("vT", 203.5, [P, T])
        PS = [ctx.enter_context(nc.psum_tensor(f"PS{b}", [P, 512], F32)) for b in range(8)]

        c16b = c16[:, :].bitcast(BF16)
        ident_b, before_b, ones_b = c16b[:, 0:P], c16b[:, P:2 * P], c16b[:, 2 * P:3 * P]
        HTf = HT[:, :, :].rearrange("p a b -> p (a b)")
        HTQf = HTQ[:, :, :].rearrange("p a b -> p (a b)")

        def cut(buf, at, *dims):
            n = 1
            for d in dims:
                n *= d
            ap = buf[:, at:at + n]
            if len(dims) == 2:
                return ap.rearrange("p (a b) -> p a b", a=dims[0])
            if len(dims) == 3:
                return ap.rearrange("p (a b c) -> p a b c", a=dims[0], b=dims[1])
            if len(dims) == 4:
                return ap.rearrange("p (a b c d) -> p a b c d", a=dims[0], b=dims[1], c=dims[2])
            return ap

        XN = {"a": cut(HTQf, 0, NT, D), "f0": cut(HTQf, 0, NT, D), "f1": cut(HTQf, 0, NT, D),
              "kv": cut(SC, 0, NT, D), "out": cut(WR, 0, NT, D)}
        w_in_sb = [cut(WR, b * 2048, KT, 2, P) for b in range(2)]
        b_out_sb = cut(WR, 5 * 4096, D)
        W_U = PAD + T
        upad = [cut(SC, b * W_U, W_U) for b in range(2)]
        o = 2 * W_U
        sig = [cut(SC, o + b * T, T) for b in range(2)]
        o += 2 * T
        accv = [cut(SC, o + b * T, T) for b in range(2)]
        o += 2 * T
        accp = [cut(SC, o + b * T, T) for b in range(2)]
        o += 2 * T
        lnsq = [cut(SC, o + b * T, T) for b in range(2)]
        o += 2 * T
        onesf = cut(SC, o, P)
        o += P
        cv = cut(SC, o, CONV_COLS)
        o += CONV_COLS
        taps_v = [cut(SC, o + b * 32, 32) for b in range(2)]
        o += 64
        ctap = [cut(SC, o + b * T, T) for b in range(NPROD - 2)] + lnsq
        o += (NPROD - 2) * T
        lnstd = cut(SC, o, T)
        o += T
        assert o <= 7680 - KT * (EG + E)
        wg = [cut(WR, b * 4096, KT, F) for b in range(2)]
        wu = [cut(WR, (2 + b) * 4096, KT, F) for b in range(2)]
        wd = [cut(WR, (4 + b) * 4096, FT, D) for b in range(2)]
        xg = [cut(SC, b * D, D) for b in range(2)]
        xgT = [cut(SC, 2 * D + b * D, KT, P) for b in range(2)]
        sil = cut(SC, 4096, F)
        hid = cut(SC, 4608, F)
        hidT = cut(SC, 5120, FT, P)
        yst = [cut(SC, 5632 + b * D, D) for b in range(2)]
        rt = cut(SC, 7680 - KT * (EG + E), KT, EG + E)
        yg = [cut(HTf, 0, NT, D), cut(SC, 0, NT, D)]
        o = 0

        def rs(*dims, dt=F32):
            nonlocal o
            n = 1
            for d in dims:
                n *= d
            ap = cut(HTQf, o, *dims)
            o += n
            return ap.bitcast(dt) if dt != F32 else ap

        lg = rs(NT, EG + E)
        gmax, gsum = rs(NT, 1), rs(NT, 1)
        gexp = rs(NT, EG)
        gsel = rs(NT, EG)
        prod = rs(NT, EG, EG)
        sel = rs(NT, EG)
        top = [rs(NT, 1) for _ in range(2)]
        esel = [rs(NT, EG) for _ in range(2)]
        pick = rs(NT, 1)
        tmp4 = rs(NT, EG)
        hot_all = rs(2 * NT, E)
        hot = [hot_all[:, k * NT:(k + 1) * NT, :].rearrange("p n (g e) -> p n g e", g=EG) for k in range(2)]
        both = cut(HTQf, o, NT * E // 2).bitcast(BF16).rearrange("p (a b) -> p a b", a=NT)
        o += NT * E // 2
        rank = rs(NT, E)
        count = rs(E)
        wt = [rs(NT, 1) for _ in range(2)]
        rk = rs(2 * NT)
        ge = rs(2 * NT, MAXC + 1)
        inblk = rs(2 * NT, MAXC)
        col4 = rs(2 * NT, MAXC)
        col = rs(2 * NT)
        hr = rs(2 * NT, E)
        big = rs(2 * NT, MAXC, E)
        over = rs(MAXC - 1, E)
        pos = rs(MAXC, E)
        nover = rs(1)
        gadd = rs(2 * NT)
        half4 = rs(4)
        match = rs(XB, MAXC - 1, E)
        blk_e = rs(E + XB, dt=I32)
        blk_f = rs(XB)
        last_i = rs(2, dt=I32)
        two_i = rs(2, dt=I32)
        parity = rs(4)
        slot_ids = rs(SLOTS, dt=U32)
        src_ids = rs(SLOTS, dt=U32)
        src_f = rs(SLOTS)
        scol = [rs(1, dt=U32) for _ in range(2)]
        dcol = [rs(1, dt=U32) for _ in range(2)]
        ones48 = rs(MAXC - 1, E)
        limits = rs(MAXC + 1)
        xcols = rs(XB)
        tie_w = rs(EG)
        eidx = rs(E)
        assert o <= 4096
        o = 4096

        def ms(*dims, dt=F32):
            nonlocal o
            n = 1
            for d in dims:
                n *= d
            w = n * mybir.dt.size(dt) // 4
            ap = SC[:, o:o + w]
            o += w
            ap = ap.bitcast(dt) if dt != F32 else ap
            names = "abcd"[:len(dims)]
            return ap if len(dims) == 1 else ap.rearrange(f"p ({' '.join(names)}) -> p {' '.join(names)}", **dict(zip(names, dims)))

        seq_i, seq = ms(P, dt=I32), ms(P)
        part_i = ms(2 * NT, dt=I32)
        what = ms(2 * NT, 4)
        rk_hot = ms(2 * NT, P, dt=BF16)
        col_hot = ms(2 * NT, SLOTS)
        col_what = ms(2 * NT, 4, SLOTS, dt=BF16)
        found = ms(4, SLOTS)
        assert o <= 5632
        Kh = [KQ[:, h, :, :] for h in range(2)]
        Qh = [KQ[:, 2 + h, :, :] for h in range(2)]
        Pm = [Pm2[:, h * 1920:(h + 1) * 1920] for h in range(2)]
        masks_b = masks[:, :, :].bitcast(BF16)
        fin_g = cut(WR, 5 * 4096, D)

        x_in = [sem(f"x_in{n}") for n in range(NT)]
        const_in, cvec_in, bout_in, wout_in = sem("const_in"), sem("cvec_in"), sem("bout_in"), sem("wout_in")
        norms = ("a", "f0", "kv", "f1", "out")
        half = KT // 2
        sq_done = Count(sem("sq_done"), norms, [NT] * 5)
        var_ready = Count(sem("var_ready"), norms, [NT] * 5)
        std_ready = Count(sem("std_ready"), norms, [NT] * 5)
        xn_ready = Count(sem("xn_ready"), norms, [NT] * 4 + [0])
        xT_ready = Count(sem("xT_ready"), norms, [KT] * 4 + [0])
        ht_act = Count(sem("ht_act"), norms, [half, half, 2 * KT, half, 0])
        ht_dve = Count(sem("ht_dve"), norms, [half, half, 2 * KT, half, 0])
        x_upd = Count(sem("x_upd"), norms, [0] + [NT] * 4)
        v_steps, p_steps = sem("v_steps"), sem("p_steps")
        win_in = [sem(f"win_in{b}") for b in range(2)]
        u_mm = [sem(f"u_mm{b}") for b in range(2)]
        sig_done = [sem(f"sig_done{b}") for b in range(2)]
        glu_done = [sem(f"glu_done{b}") for b in range(2)]
        pool_conv = [sem(f"pool_conv{b}") for b in range(2)]
        conv_done = [sem(f"conv_done{b}") for b in range(2)]
        bout_added, mean_mm, ln_d, ln_sq, var_mm = (sem(s) for s in ("bout_added", "mean_mm", "ln_d", "ln_sq", "var_mm"))
        lnvar_ready, lnstd_ready, ln_n, silu_done, wout_mm = (sem(s) for s in ("lnvar_ready", "lnstd_ready", "ln_n", "silu_done", "wout_mm"))
        wo_lead, silu_lead, silu_trail = sem("wo_lead"), sem("silu_lead"), sem("silu_trail")
        conv_init, prod_done = sem("conv_init"), sem("prod_done")
        L2 = range(2)
        xn_stored = Count(sem("xn_stored"), L2, [NT * 16] * 2)
        rt_in = Count(sem("rt_in"), L2, [16] * 2)
        iota_done = Count(sem("iota_done"), L2, [4] * 2)
        src_ready = Count(sem("src_ready"), L2, [1] * 2)
        logit_mm = Count(sem("logit_mm"), L2, [1] * 2)
        gdiff = Count(sem("gdiff"), L2, [1] * 2)
        gexp_done = Count(sem("gexp_done"), L2, [2] * 2)
        both_ready = Count(sem("both_ready"), L2, [1] * 2)
        rank_mm = Count(sem("rank_mm"), L2, [1] * 2)
        routed = Count(sem("routed"), L2, [1] * 2)
        hot_ready = Count(sem("hot_ready"), L2, [1] * 2)
        slots_mm = Count(sem("slots_mm"), L2, [1] * 2)
        scol_done = [sem(f"scol_done{l}") for l in L2]
        dcol_done = [sem(f"dcol_done{l}") for l in L2]
        gathered = [[sem(f"gathered{l}{b}") for b in range(2)] for l in L2]
        xgT_mm = [[sem(f"xgT_mm{l}{b}") for b in range(2)] for l in L2]
        xgT_done = [[sem(f"xgT_done{l}{b}") for b in range(2)] for l in L2]
        wg_in = [[sem(f"wg_in{l}{b}") for b in range(2)] for l in L2]
        wu_in = [[sem(f"wu_in{l}{b}") for b in range(2)] for l in L2]
        wd_in = [[sem(f"wd_in{l}{b}") for b in range(2)] for l in L2]
        gate_mm = [sem(f"gate_mm{l}") for l in L2]
        up_mm = [sem(f"up_mm{l}") for l in L2]
        hT_mm = [sem(f"hT_mm{l}") for l in L2]
        down_mm = [sem(f"down_mm{l}") for l in L2]
        sil_done = [sem(f"sil_done{l}") for l in L2]
        hid_done = [sem(f"hid_done{l}") for l in L2]
        hidT_done = [sem(f"hidT_done{l}") for l in L2]
        y_done = [sem(f"y_done{l}") for l in L2]
        gh_done, gl_done, uh_done, ul_done, xh_done, xl_done, y_free = (
            [sem(f"{name}{l}") for l in L2] for name in ("gh_done", "gl_done", "uh_done", "ul_done", "xh_done", "xl_done", "y_free"))
        y_stored = [[sem(f"y_stored{l}{b}") for b in range(2)] for l in L2]
        y_back = [sem(f"y_back{n}") for n in range(NT)]
        att_const = sem("att_const")
        wu_raw = [sem(f"wu_raw{s}") for s in range(NU)]
        wh_done, wl_done, unit_mm, att_init = (sem(s) for s in ("wh_done", "wl_done", "unit_mm", "att_init"))
        pairs_done, row_done = sem("pairs_done"), sem("row_done")
        rope_ab_done, hi_done, oTh_done, oTl_done, o_free = (sem(s) for s in ("rope_ab_done", "hi_done", "oTh_done", "oTl_done", "o_free"))
        rope_done, v_done = (sem(s) for s in ("rope_done", "v_done"))
        s1_mm, max_done, row_mm, vT_done, v_mm = (sem(s) for s in ("s1_mm", "max_done", "row_mm", "vT_done", "v_mm"))
        s2_mm, exp_done, pv_mm, oT_done, wo_mm = (sem(s) for s in ("s2_mm", "exp_done", "pv_mm", "oT_done", "wo_mm"))
        fin_in, y_ready, out_stored = sem("fin_in"), sem("y_ready"), sem("out_stored")

        block = ctx.enter_context(nc.Block())

        @block.sync
        def _(sp):
            for n in range(NT):
                sp.dma_start(X[:, n, :], x[0, n * P:(n + 1) * P, :]).then_inc(x_in[n], 16)
            for b in range(2):
                sp.dma_start(w_in_sb[b].rearrange("p a b c -> p (a b c)"), a["w_in"][b]).then_inc(win_in[b], 16)

            def expert_load(l, j, b, dst, name, s):
                src = a[name][bass.ds(j, 1), :, :].rearrange("e p n -> (e p) n") if not isinstance(j, int) else a[name][j]
                sp.dma_start(dst[b].rearrange("p a b -> p (a b)"), src).then_inc(s[l][b], 16)

            for c in range(2, KT):
                sp.wait_ge(u_mm[c % 2], c // 2)
                sp.dma_start(w_in_sb[c % 2].rearrange("p a b c -> p (a b c)"), a["w_in"][c]).then_inc(win_in[c % 2], 16)
                if c == 2:
                    expert_load(0, 1, 1, wg, "w_gate", wg_in)
                if c in (3, 4):
                    expert_load(0, c - 3, c - 3, wu, "w_up", wu_in)
                if c == 6:
                    sp.dma_start(WO[:, :, :], a["w_out"]).then_inc(wout_in, 16)
            for b in range(2):
                sp.wait_ge(u_mm[b], KT // 2)
            expert_load(0, 0, 0, wg, "w_gate", wg_in)

            def moe_sp(l):
                for n in range(NT):
                    sp.wait_ge(xn_ready.sem, xn_ready.at(f"f{l}", n + 1))
                    sp.dma_start(xn_dram[l][n * P:(n + 1) * P, :], XN[f"f{l}"][:, n, :]).then_inc(xn_stored.sem, 16)
                if l == 0:
                    sp.wait_ge(wout_mm, 2 * NT)
                    for b in range(2):
                        expert_load(0, b, b, wd, "w_down", wd_in)
                if l == 1:
                    for b in range(2):
                        expert_load(1, E + b, b, wg, "w_gate", wg_in)
                        expert_load(1, E + b, b, wu, "w_up", wu_in)
                    expert_load(1, E + 1, 1, wd, "w_down", wd_in)
                    expert_load(1, E, 0, wd, "w_down", wd_in)
                sp.wait_ge(routed.sem, routed.at(l, 1))
                last = sp.value_load(last_i[0:1, 0:1], min_val=E // 2 - 1, max_val=(E + XB) // 2 - 1)
                two = sp.value_load(two_i[0:1, 0:1], min_val=0, max_val=1)
                seconds = sp.value_load(two_i[0:1, 1:2], min_val=E // 2 * 16, max_val=(E + XB) // 2 * 16)

                before = sp.value_load(last_i[0:1, 1:2], min_val=E // 2 - 2, max_val=(E + XB) // 2 - 2)

                def expert_loads(i, bs, uses):
                    for b in bs:
                        j = sp.value_load(blk_e[0:1, bass.ds(2 * i + b, 1)], min_val=0, max_val=E - 1) + l * E
                        for dst, name, s, used in ((wg, "w_gate", wg_in, gate_mm), (wu, "w_up", wu_in, up_mm), (wd, "w_down", wd_in, down_mm)):
                            sp.wait_ge(used[l], uses + b)
                            expert_load(l, j, b, dst, name, s)

                with sp.Fori(1, last) as i:
                    expert_loads(i, (0, 1), 2 * i - 1)
                expert_loads(last, (0,), 2 * before + 1)
                with sp.If(two > 0):
                    expert_loads(last, (1,), 2 * before + 1)
                sp.wait_ge(y_stored[l][0], (last + 1) * 16)
                sp.wait_ge(y_stored[l][1], seconds)
                for n in range(NT):
                    for k in range(2):
                        sp.dma_start(yg[k][:, n, :], y_dram[l][k * T + n * P:k * T + (n + 1) * P, :]).then_inc(y_back[n], 16)

            moe_sp(0)
            def unit(src, s):
                sp.dma_start(wraw[:, s, :], src).then_inc(wu_raw[s], 16)

            for m in range(NU):
                unit(a["w_qkv"][m], m)
            sp.dma_start(rope_t[:, :, :], a["rope"]).then_inc(att_const, 16)
            sp.wait_ge(xT_ready.sem, xT_ready.at("kv", KT))
            sp.dma_start(masks[:, :, :].rearrange("p a b -> p (a b)"), a["masks"]).then_inc(att_const, 16)
            with sp.Fori(0, NP_HEADS - 1) as i:
                for u in range(9):
                    sp.wait_ge(wl_done, 9 * i + (u + 1))
                    unit(a["w_qkv"][bass.ds(9 * i + (u + NU), 1), :, :].rearrange("e p n -> (e p) n"), u % NU)
            for m in range(9 * (NP_HEADS - 1) + NU, 9 * NP_HEADS + KT):
                sp.wait_ge(wl_done, m - NU + 1)
                unit(a["w_qkv"][m] if m < 9 * NP_HEADS else a["w_o"][m - 9 * NP_HEADS], m % NU)
            sp.wait_ge(oT_done, 2 * NP_HEADS)
            sp.dma_start(rt.rearrange("p a b -> p (a b)"), a["router"][1]).then_inc(rt_in.sem, 16)
            sp.wait_ge(wo_mm, 2 * NT)
            moe_sp(1)
            sp.dma_start(fin_g, a["final_norm"].to_broadcast([P, D])).then_inc(fin_in, 16)
            for n in range(NT):
                sp.wait_ge(y_ready, n + 1)
                sp.dma_start(out[0, n * P:(n + 1) * P, :], XN["out"][:, n, :]).then_inc(out_stored, 16)
            sp.wait_ge(out_stored, NT * 16)

        @block.gpsimd
        def _(pool):
            steps = Steps(pool, p_steps)
            for c, s in enumerate(pool_conv + y_free):
                nc.gpsimd.memset(spare[:, c:c + 1], 0.0).then_inc(s, 1)
            nc.gpsimd.memset(onesf, 1.0 / D)
            for b in range(2):
                last = nc.gpsimd.memset(upad[b][:, 0:PAD], 0.0)
            last.then_inc(conv_init, 1)
            pool.wait_ge(bout_in, 16)
            for n in range(NT):
                pool.wait_ge(xn_ready.sem, xn_ready.at("a", n + 1))
                nc.gpsimd.tensor_tensor(X[:, n, :], X[:, n, :], b_out_sb, ALU.add).then_inc(bout_added, 1)
            for c in range(POOL_TAPS - 2):
                steps.mark(nc.gpsimd.memset(accp[0][:, c:c + 1], 0.0))
            steps.wait()
            with pool.Fori(0, KT // 2) as i:
                steps.enter(i, 2 * (POOL_TAPS - 2))
                for b in range(2):
                    for t in range(1, POOL_TAPS):
                        pool.wait_ge(prod_done, (2 * i + b) * POOL_TAPS + (t + 1))
                        if t == 1:
                            pool.wait_ge(conv_done[b], i + 1)
                            ins = nc.gpsimd.tensor_tensor(accp[b], ctap[0], ctap[1], ALU.add)
                        else:
                            ins = nc.gpsimd.tensor_tensor(accp[b], accp[b], ctap[t % NPROD], ALU.add)
                        if t < POOL_TAPS - 1:
                            steps.step(ins)
                        else:
                            ins.then_inc(pool_conv[b], 1)
                steps.leave(KT // 2)

            def moe_pool(l):
                pool.wait_ge(xn_stored.sem, xn_stored.at(l, NT * 16))
                pool.wait_ge(xT_ready.sem, xT_ready.at(f"f{l}", KT))
                nc.gpsimd.iota(seq_i, pattern=[[1, P]], base=0, channel_multiplier=0).then_inc(iota_done.sem, 1)
                nc.gpsimd.iota(part_i, pattern=[[0, 2 * NT]], base=0, channel_multiplier=1).then_inc(iota_done.sem, 1)
                for b in range(2):
                    nc.gpsimd.memset(xg[b], 0.0).then_inc(iota_done.sem, 1)
                pool.wait_ge(iota_done.sem, iota_done.at(l, 4))
                pool.wait_ge(routed.sem, routed.at(l, 1))
                last = pool.value_load(last_i[0:1, 0:1], min_val=E // 2 - 1, max_val=(E + XB) // 2 - 1)
                two = pool.value_load(two_i[0:1, 0:1], min_val=0, max_val=1)
                before = pool.value_load(last_i[0:1, 1:2], min_val=E // 2 - 2, max_val=(E + XB) // 2 - 2)

                def gather(b, n):
                    nc.gpsimd.tensor_copy(scol[b], src_ids[:, bass.ds(2 * n + b, 1)]).then_inc(scol_done[l], 1)
                    if not isinstance(n, int) or n > 0:
                        pool.wait_ge(xgT_mm[l][b], n)
                    pool.wait_ge(scol_done[l], 2 * n + b + 1)
                    nc.gpsimd.tensor_tensor(idle[:, :], ident[:, 0:1], ident[:, 0:1], ALU.mult)
                    pool.indirect_dma_start(xg[b], None, xn_dram[l], bass.IndirectOffsetOnAxis(ap=scol[b], axis=0),
                                            bounds_check=T - 1, oob_is_err=False).then_inc(gathered[l][b], 16)

                def scatter(b, n):
                    nc.gpsimd.tensor_copy(dcol[b], slot_ids[:, bass.ds(2 * n + b, 1)]).then_inc(dcol_done[l], 1)
                    pool.wait_ge(y_done[l], 2 * n + (b + 2))
                    pool.wait_ge(dcol_done[l], 2 * n + (b + 1))
                    nc.gpsimd.tensor_tensor(idle[:, :], ident[:, 0:1], ident[:, 0:1], ALU.mult)
                    pool.indirect_dma_start(y_dram[l], bass.IndirectOffsetOnAxis(ap=dcol[b], axis=0), yst[b], None,
                                            bounds_check=2 * T - 1, oob_is_err=False).then_inc(y_stored[l][b], 16)

                pool.wait_ge(src_ready.sem, src_ready.at(l, 1))
                for b in range(2):
                    gather(b, 0)

                def stored(n):
                    for b in range(2):
                        pool.wait_ge(y_stored[l][b], n * 16)
                    nc.gpsimd.tensor_tensor(spare[:, 7:8], ident[:, 0:1], ident[:, 0:1], ALU.mult).then_inc(y_free[l], 1)

                def pair(i, more):
                    if not isinstance(i, int):
                        stored(i)
                    for b in range(2):
                        if more:
                            pool.wait_ge(gathered[l][b], (i + 2) * 16)
                            gather(b, i + 2)
                        scatter(b, i)

                for b in range(2):
                    pool.wait_ge(gathered[l][b], 16)
                    gather(b, 1)
                pair(0, True)
                with pool.Fori(1, before) as i:
                    pair(i, True)
                pair(before, False)
                stored(last)
                scatter(0, last)
                with pool.If(two > 0):
                    scatter(1, last)

            moe_pool(0)
            pool.wait_ge(down_mm[0], E)
            for n in range(NT):
                pool.wait_ge(y_back[n], 32)
            steps.step(nc.gpsimd.memset(Vs[:, :, :, :, :], 1.0))
            for h in range(2):
                steps.step(nc.gpsimd.memset(Kh[h][HEAD:HEAD + 1, :, :], 1.0))
            nc.gpsimd.memset(idle[:, :], 0.0).then_inc(att_init, 1)
            with pool.Fori(0, NP_HEADS) as i:
                for t in range(6):
                    dst, g = (Qh, t) if t < 3 else (Kh, t - 3)
                    pool.wait_ge(rope_ab_done, 6 * i + (t + 1))
                    if t == 0:
                        pool.wait_ge(pairs_done, i + 1)
                    for h in range(2):
                        rows = slice(h * HEAD, (h + 1) * HEAD)
                        ins = nc.gpsimd.tensor_tensor(dst[h][0:HEAD, g, :], rope_ab[rows, 2 * (t % 2), :], rope_ab[rows, 2 * (t % 2) + 1, :], ALU.add)
                        ins.then_inc(rope_done, 1)
            moe_pool(1)

        @block.scalar
        def _(act):
            act.dma_start(ident[:, :], a["ident"]).then_inc(const_in, 16)
            act.dma_start(vn[:, :], a["norm_vecs"]).then_inc(const_in, 16)
            act.dma_start(c16[:, :], a["c16"]).then_inc(const_in, 16)
            act.dma_start(cv, a["conv_vecs"]).then_inc(cvec_in, 16)
            act.dma_start(b_out_sb, a["b_out"].to_broadcast([P, D])).then_inc(bout_in, 16)
            act.dma_start(rt.rearrange("p a b -> p (a b)"), a["router"][0]).then_inc(rt_in.sem, 16)

            def norm_act(k):
                def square(n):
                    if k == "a":
                        act.wait_ge(x_in[n], 16)
                    else:
                        act.wait_ge(x_upd.sem, x_upd.at(k, n + 1))
                    nc.scalar.activation(XN[k][:, n, :], X[:, n, :], ACT.Square, accum_out=ss[:, n:n + 1]).then_inc(sq_done.sem, 1)

                square(0)
                for n in range(NT):
                    if n + 1 < NT:
                        square(n + 1)
                    act.wait_ge(var_ready.sem, var_ready.at(k, n + 1))
                    nc.scalar.activation(rstd[:, n:n + 1], ss[:, n:n + 1], ACT.Sqrt).then_inc(std_ready.sem, 1)
                if k == "out":
                    return
                if k == "kv":
                    for s in range(NU):
                        leading(s, 16, s, None)
                    for q, kt in KV_ORDER:
                        act.wait_ge(xT_ready.sem, xT_ready.at(k, kt + 1))
                        if not q:
                            act.wait_ge(ht_dve.sem, ht_dve.at(k, KV_ORDER.index((1, kt)) + 1))
                        dst, v = (HQh, V_NORM["q"]) if q else (HTh, V_NORM["kv"])
                        nc.scalar.activation(dst[:, kt, :], PS[kt][:, :], ACT.Copy, scale=vn[:, v + kt:v + kt + 1]).then_inc(ht_act.sem, 1)
                    return
                for kt in range(KT):
                    if kt % 2 == 0:
                        act.wait_ge(xT_ready.sem, xT_ready.at(k, kt + 1))
                        nc.scalar.activation(HT[:, kt, :], PS[kt][:, :], ACT.Copy, scale=vn[:, V_NORM[k] + kt:V_NORM[k] + kt + 1]).then_inc(ht_act.sem, 1)

            act.wait_ge(const_in, 48)
            for c, s in enumerate(y_done):
                nc.scalar.activation(spare[:, 4 + c:5 + c], ident[:, 0:1], ACT.Copy).then_inc(s, 1)
            norm_act("a")
            act.wait_ge(cvec_in, 16)

            def sigmoid(b, n):
                act.wait_ge(u_mm[b], n + 1)
                act.wait_ge(glu_done[b], n + 1)
                nc.scalar.activation(sig[b], PS[2 * b + 1][:, :], ACT.Sigmoid,
                                     bias=cv[:, bass.ds(2 * n + b + (C_BIN + KT), 1)]).then_inc(sig_done[b], 1)

            def products(b, i, ahead):
                act.wait_ge(glu_done[b], i + 2)
                for t in range(POOL_TAPS):
                    before = (POOL_TAPS - 1 - t) // NPROD * NPROD + t
                    if t >= NPROD:
                        act.wait_ge(p_steps, (2 * i + b + 1) * (POOL_TAPS - 2) + max(1, t - NPROD))
                    elif before == POOL_TAPS - 1:
                        act.wait_ge(pool_conv[1 - b], i + (b + 1))
                    else:
                        act.wait_ge(p_steps, (2 * i + b) * (POOL_TAPS - 2) + before)
                    tap = CONV - POOL_TAPS + t
                    nc.scalar.activation(ctap[t % NPROD], upad[b][:, tap:tap + T], ACT.Copy,
                                         scale=cv[:, bass.ds((2 * i + b) * CONV + (C_WDW + tap), 1)]).then_inc(prod_done, 1)
                    if ahead and t == 2:
                        sigmoid(*ahead)

            sigmoid(0, 0)
            with act.Fori(0, KT // 2 - 1) as i:
                products(0, i, (1, i))
                products(1, i, (0, i + 1))
            products(0, KT // 2 - 1, (1, KT // 2 - 1))
            products(1, KT // 2 - 1, None)
            act.wait_ge(wout_in, 16)
            act.wait_ge(bout_added, NT)
            for c in range(KT):
                nc.scalar.activation(WOh[:, c, :], WO[:, c, :], ACT.Copy).then_inc(wo_lead, 1)
            for c in range(KT):
                act.wait_ge(ln_d, c + 1)
                if c >= 2:
                    act.wait_ge(var_mm, c - 1)
                nc.scalar.activation(lnsq[c % 2], HTQ[:, c, :], ACT.Square).then_inc(ln_sq, 1)
            act.wait_ge(lnvar_ready, 1)
            nc.scalar.activation(lnstd, lnstd, ACT.Sqrt).then_inc(lnstd_ready, 1)
            for c in range(KT):
                act.wait_ge(ln_n, c + 1)
                nc.scalar.activation(HTQ[:, c, :], HTQ[:, c, :], ACT.Silu, bias=cv[:, C_LNB + c:C_LNB + c + 1],
                                     scale=cv[:, C_LNG + c:C_LNG + c + 1]).then_inc(silu_done, 1)
                act.wait_ge(silu_done, c + 1)
                nc.scalar.activation(HTh[:, c, :], HTQ[:, c, :], ACT.Copy).then_inc(silu_lead, 1)

            def moe_act(l):
                norm_act(f"f{l}")
                act.wait_ge(gdiff.sem, gdiff.at(l, 1))
                nc.scalar.activation(gexp, gexp, ACT.Exp).then_inc(gexp_done.sem, 1)
                nc.scalar.activation(pick, pick, ACT.Exp).then_inc(gexp_done.sem, 1)

                def lead(src, dst, w_in, done, n):
                    act.wait_ge(w_in, n * 16)
                    for q in range(2):
                        kts = slice(q * KT // 2, (q + 1) * KT // 2)
                        nc.scalar.activation(dst[:, kts, :], src[:, kts, :], ACT.Copy).then_inc(done, 1)

                def gate_lead(b, n, used):
                    if used is not None:
                        act.wait_ge(gate_mm[l], used)
                    lead(wg[b], wgh, wg_in[l][b], gh_done[l], n)

                def up_lead(b, n, used):
                    if used is not None:
                        act.wait_ge(up_mm[l], used)
                    lead(wu[b], wuh, wu_in[l][b], uh_done[l], n)

                def rows_lead(b, n):
                    act.wait_ge(xgT_done[l][b], n)
                    nc.scalar.activation(xgh[b][:, :, :], xgT[b], ACT.Copy).then_inc(xh_done[l], 1)

                gate_lead(0, 1, None)
                up_lead(0, 1, None)
                for b in range(2):
                    rows_lead(b, 1)
                act.wait_ge(routed.sem, routed.at(l, 1))
                two = act.value_load(two_i[0:1, 0:1], min_val=0, max_val=1)
                last = act.value_load(last_i[0:1, 0:1], min_val=E // 2 - 1, max_val=(E + XB) // 2 - 1)

                def pair(i, more):
                    def silu_gate(b):
                        act.wait_ge(gate_mm[l], 2 * i + (b + 1))
                        act.wait_ge(hid_done[l], 2 * i + (b + 1))
                        nc.scalar.activation(sil, PS[0][:, :], ACT.Silu).then_inc(sil_done[l], 1)

                    def store_y(b):
                        act.wait_ge(down_mm[l], 2 * i + (b + 1))
                        act.wait_ge(y_free[l], i + 1)
                        nc.scalar.activation(yst[b][:, 0:512], PS[3][:, :], ACT.Copy)
                        nc.scalar.activation(yst[b][:, 512:1024], PS[4][:, :], ACT.Copy).then_inc(y_done[l], 1)

                    silu_gate(0)
                    if more:
                        gate_lead(1, i + 1, 2 * i + 1)
                        up_lead(1, i + 1, 2 * i + 1)
                        silu_gate(1)
                        gate_lead(0, i + 2, 2 * i + 2)
                        rows_lead(0, i + 2)
                        up_lead(0, i + 2, 2 * i + 2)
                        store_y(0)
                        rows_lead(1, i + 2)
                        store_y(1)
                    else:
                        with act.If(two > 0):
                            gate_lead(1, i + 1, 2 * i + 1)
                            up_lead(1, i + 1, 2 * i + 1)
                            silu_gate(1)
                        store_y(0)
                        with act.If(two > 0):
                            store_y(1)

                with act.Fori(0, last) as i:
                    pair(i, True)
                pair(last, False)

            moe_act(0)
            def leading(s, n, m, used):
                act.wait_ge(wu_raw[s], n)
                if used is not None:
                    act.wait_ge(unit_mm, used)
                nc.scalar.activation(wh[:, s, :], wraw[:, s, :], ACT.Copy).then_inc(wh_done, 1)

            norm_act("kv")
            act.wait_ge(att_init, 1)
            with act.Fori(0, NP_HEADS) as i:
                def copy_leading(h):
                    if h == 0:
                        act.wait_ge(pairs_done, i + 1)
                        act.wait_ge(rope_done, 12 * i + 6)
                    else:
                        act.wait_ge(rope_done, 12 * i + 12)
                        act.wait_ge(s1_mm, 8 * i + 4)
                    nc.scalar.activation(QKh[0:HEAD, 0, :, :], Qh[h][0:HEAD, :, :], ACT.Copy)
                    if h == 0:
                        act.wait_ge(rope_done, 12 * i + 10)
                        nc.scalar.activation(QKh[0:HEAD, 1, 0:2, :], Kh[h][0:HEAD, 0:2, :], ACT.Copy)
                        act.wait_ge(rope_done, 12 * i + 11)
                        nc.scalar.activation(QKh[0:HEAD, 1, 2, :], Kh[h][0:HEAD, 2, :], ACT.Copy).then_inc(hi_done, 1)
                    else:
                        nc.scalar.activation(QKh[0:HEAD, 1, :, :], Kh[h][0:HEAD, :, :], ACT.Copy).then_inc(hi_done, 1)

                for u in range(9):
                    g = u - 6
                    if g >= 0:
                        act.wait_ge(unit_mm, 9 * i + (u + 1))
                        if g > 0:
                            act.wait_ge(v_mm, 3 * i + g)
                        nc.scalar.activation(vT[:, :], PS[2 + g % 2][:, :], ACT.Copy).then_inc(vT_done, 1)
                    leading(u % NU, 48 * i + 16 * (u // NU + 2), u, 9 * i + (u + 1))
                    if u == 5:
                        copy_leading(0)
                    if u == 6:
                        copy_leading(1)
                    if g >= 0:
                        act.wait_ge(v_mm, 3 * i + (g + 1))
                        nc.scalar.activation(Vs[:, g, :, :, 0:HEAD], PS[2 + g % 2][:, :].rearrange("p (n h d) -> p n h d", n=NT, h=2),
                                             ACT.Copy).then_inc(v_done, 1)
                for h in range(2):
                    for k in range(4):
                        act.wait_ge(s2_mm, 8 * i + (4 * h + k + 1))
                        w = 384 if k == 3 else 512
                        nc.scalar.activation(Pm[h][:, k * 512:k * 512 + w], PS[4 + k][:, 0:w], ACT.Exp).then_inc(exp_done, 1)
            act.wait_ge(oT_done, 2 * NP_HEADS)
            for c in range(KT):
                nc.scalar.activation(HQh[:, c, :], oT[:, c, :], ACT.Copy).then_inc(oTh_done, 1)
            for m in range(9 * NP_HEADS + NU, 9 * NP_HEADS + KT):
                leading(m % NU, 16 * (m // NU + 1), m, m - NU + 1)
            moe_act(1)
            norm_act("out")

        @block.vector
        def _(dve):
            steps = Steps(dve, v_steps)
            V = nc.vector
            V.memset(tick[0:1, :], 0.0).then_inc(pairs_done, 1)
            V.memset(rowt[0:1, :], 0.0).then_inc(row_done, 1)
            for c, s in enumerate(hid_done + glu_done + conv_done):
                V.memset(spare[:, 8 + c:9 + c], 0.0).then_inc(s, 1)

            def norm_dve(k, update=None):
                if update:
                    update(0)
                for n in range(NT):
                    if update and n + 1 < NT:
                        update(n + 1)
                    one = slice(n, n + 1)
                    dve.wait_ge(sq_done.sem, sq_done.at(k, n + 1))
                    V.tensor_scalar(ss[:, one], ss[:, one], 1.0 / D, EPS, ALU.mult, ALU.add).then_inc(var_ready.sem, 1)
                    dve.wait_ge(std_ready.sem, std_ready.at(k, n + 1))
                    steps.step(V.reciprocal(rstd[:, one], rstd[:, one]))
                    if k == "out":
                        if n == 0:
                            dve.wait_ge(fin_in, 16)
                        V.scalar_tensor_tensor(XN[k][:, n, :], X[:, n, :], rstd[:, one], fin_g, ALU.mult, ALU.mult).then_inc(y_ready, 1)
                    else:
                        V.tensor_scalar(XN[k][:, n, :], X[:, n, :], rstd[:, one], None, ALU.mult).then_inc(xn_ready.sem, 1)
                if k == "out":
                    return
                if k == "kv":
                    for s in range(NU):
                        trailing(s, s + 1)
                    for n, (q, kt) in enumerate(KV_ORDER):
                        dst, hi, v = (HQl, HQh, V_NORM["q"]) if q else (HTl, HTh, V_NORM["kv"])
                        dve.wait_ge(ht_act.sem, ht_act.at(k, n + 1))
                        V.scalar_tensor_tensor(dst[:, kt, :], PS[kt][:, :], vn[:, v + kt:v + kt + 1], hi[:, kt, :].bitcast(F32),
                                               ALU.mult, ALU.subtract).then_inc(ht_dve.sem, 1)
                else:
                    for kt in range(1, KT, 2):
                        dve.wait_ge(xT_ready.sem, xT_ready.at(k, kt + 1))
                        V.tensor_scalar(HT[:, kt, :], PS[kt][:, :], vn[:, V_NORM[k] + kt:V_NORM[k] + kt + 1], None, ALU.mult).then_inc(ht_dve.sem, 1)

            dve.wait_ge(const_in, 48)
            norm_dve("a")
            dve.wait_ge(cvec_in, 16)
            dve.wait_ge(conv_init, 1)
            nv = CONV - POOL_TAPS
            per = 2 * (1 + nv + 1)

            def gated(b, n):
                dve.wait_ge(sig_done[b], n + 1)
                dve.wait_ge(pool_conv[b], n + 1)
                V.scalar_tensor_tensor(upad[b][:, PAD:PAD + T], PS[2 * b][:, :], cv[:, bass.ds(2 * n + b + C_BIN, 1)], sig[b],
                                       ALU.add, ALU.mult).then_inc(glu_done[b], 1)

            def taps(b, i, ahead):
                steps.step(V.tensor_copy(taps_v[b][:, 0:nv], cv[:, bass.ds((2 * i + b) * CONV + C_WDW, nv)]))
                dve.wait_ge(glu_done[b], i + 2)
                steps.mark(V.tensor_scalar(accv[0], upad[b][:, 0:T], taps_v[b][:, 0:1], None, ALU.mult))
                steps.mark(V.tensor_scalar(accv[1], upad[b][:, 1:1 + T], taps_v[b][:, 1:2], cv[:, bass.ds(2 * i + b + C_BDW, 1)], ALU.mult, ALU.add))
                for t in range(2, nv):
                    steps.wait(1)
                    steps.mark(V.scalar_tensor_tensor(accv[t % 2], upad[b][:, t:t + T], taps_v[b][:, t:t + 1], accv[t % 2], ALU.mult, ALU.add))
                    if ahead and t == GLU_AT:
                        gated(*ahead)
                steps.wait()
                steps.step(V.tensor_tensor(accv[0], accv[0], accv[1], ALU.add))
                dve.wait_ge(pool_conv[b], i + 2)
                V.tensor_tensor(HTQ[:, bass.ds(2 * i + b, 1), :].rearrange("p a b -> p (a b)"), accv[0], accp[b], ALU.add).then_inc(conv_done[b], 1)

            gated(0, 0)
            with dve.Fori(0, KT // 2 - 1) as i:
                steps.enter(i, per)
                taps(0, i, (1, i))
                taps(1, i, (0, i + 1))
                steps.leave(KT // 2 - 1)
            taps(0, KT // 2 - 1, (1, KT // 2 - 1))
            taps(1, KT // 2 - 1, None)
            dve.wait_ge(mean_mm, 1)
            for b in range(2):
                dve.wait_ge(conv_done[b], KT // 2 + 1)
            for c in range(KT):
                V.tensor_tensor(HTQ[:, c, :], HTQ[:, c, :], PS[4][:, :], ALU.subtract).then_inc(ln_d, 1)

            def wo_trail(c):
                dve.wait_ge(wo_lead, c + 1)
                steps.mark(V.tensor_tensor(WOl[:, c, :], WO[:, c, :], WOh[:, c, :].bitcast(F32), ALU.subtract))

            for c in range(5):
                wo_trail(c)
            dve.wait_ge(var_mm, KT)
            V.tensor_scalar(lnstd, PS[5][:, :], EPS, None, ALU.add).then_inc(lnvar_ready, 1)
            dve.wait_ge(lnstd_ready, 1)
            steps.step(V.reciprocal(lnstd, lnstd))
            dve.wait_ge(ln_d, KT)
            for c in range(KT + 2):
                if c < KT:
                    V.tensor_tensor(HTQ[:, c, :], HTQ[:, c, :], lnstd, ALU.mult).then_inc(ln_n, 1)
                if c >= 2:
                    if c - 2 >= 5:
                        wo_trail(c - 2)
                    dve.wait_ge(silu_lead, c - 1)
                    V.tensor_tensor(HTl[:, c - 2, :], HTQ[:, c - 2, :], HTh[:, c - 2, :].bitcast(F32), ALU.subtract).then_inc(silu_trail, 1)

            def projected(n, mm, k):
                for h in range(2):
                    dve.wait_ge(mm, 2 * n + h + 1)
                    ins = V.tensor_tensor(X[:, n, h * 512:(h + 1) * 512], X[:, n, h * 512:(h + 1) * 512], PS[2 * n + h][:, :], ALU.add)
                    steps.mark(ins) if h == 0 else ins.then_inc(x_upd.sem, 1)
                steps.wait()
                dve.wait_ge(x_upd.sem, x_upd.at(k, n + 1))

            def combined(n, l):
                dve.wait_ge(y_back[n], 32 * (l + 1))
                steps.step(V.scalar_tensor_tensor(X[:, n, :], yg[0][:, n, :], wt[0][:, n, :], X[:, n, :], ALU.mult, ALU.add))
                V.scalar_tensor_tensor(X[:, n, :], yg[1][:, n, :], wt[1][:, n, :], X[:, n, :], ALU.mult, ALU.add).then_inc(x_upd.sem, 1)
                dve.wait_ge(x_upd.sem, x_upd.at(("kv", "out")[l], n + 1))

            dve.wait_ge(bout_added, NT)
            norm_dve("f0", lambda n: projected(n, wout_mm, "f0"))

            def bc(ap, *shape):
                return ap.to_broadcast(list(shape))

            def first_max(values, top1, onehot, scratch):
                steps.step(V.tensor_reduce(top1, values, AX, ALU.max))
                steps.step(V.tensor_tensor(onehot, values, bc(top1, P, NT, EG), ALU.is_equal))
                steps.step(V.tensor_tensor(onehot, onehot, tie_w.rearrange("p (a b) -> p a b", a=1).to_broadcast([P, NT, EG]), ALU.mult))
                steps.step(V.tensor_reduce(scratch, onehot, AX, ALU.max))
                steps.step(V.tensor_tensor(onehot, onehot, bc(scratch, P, NT, EG), ALU.is_equal))

            def routing(l):
                dve.wait_ge(xn_stored.sem, xn_stored.at(l, NT * 16))
                dve.wait_ge(xT_ready.sem, xT_ready.at(f"f{l}", KT))
                for g in range(EG):
                    steps.mark(V.memset(tie_w[:, g:g + 1], float(EG - g)))
                for e in range(E):
                    steps.mark(V.memset(eidx[:, e:e + 1], float(e)))
                    steps.mark(V.memset(pos[:, 0, e:e + 1], float(e)))
                for c in range(MAXC + 1):
                    steps.mark(V.memset(limits[:, c:c + 1], float(c * P)))
                for c in range(XB):
                    steps.mark(V.memset(xcols[:, c:c + 1], float(E + c)))
                steps.mark(V.memset(ones48, 1.0))
                w4 = what.rearrange("p (k n) s -> p k n s", k=2)
                steps.mark(V.memset(w4[:, :, :, 0:1], 1.0))
                for n in range(NT):
                    steps.mark(V.memset(w4[:, :, n, 1:2], float(n)))
                for k in range(2):
                    steps.mark(V.memset(w4[:, k, :, 3:4], float(k)))
                dve.wait_ge(iota_done.sem, iota_done.at(l, 2))
                steps.mark(V.tensor_copy(seq, seq_i))
                steps.mark(V.tensor_copy(what[:, :, 2:3], part_i.rearrange("p (k o) -> p k o", o=1)))
                dve.wait_ge(logit_mm.sem, logit_mm.at(l, 1))
                steps.step(V.tensor_copy(lg, PS[0][:, 0:NT * (EG + E)].rearrange("p (n e) -> p n e", n=NT)))
                lgrp, lexp = lg[:, :, 0:EG], lg[:, :, EG:EG + E]
                first_max(lgrp, gmax, gsel, gsum)
                V_g = V.tensor_tensor(gexp, lgrp, bc(gmax, P, NT, EG), ALU.subtract)
                steps.step(V_g)
                l4 = lexp.rearrange("p n (g e) -> p n e g", g=EG)
                steps.step(V.tensor_tensor(prod, l4, gsel[:, :, :].rearrange("p n (o g) -> p n o g", o=1).to_broadcast([P, NT, EG, EG]), ALU.mult))
                steps.step(V.tensor_reduce(sel[:, :, :].rearrange("p n (e o) -> p n e o", o=1), prod, AX, ALU.add))
                first_max(sel, top[0], esel[0], pick)
                steps.step(V.tensor_scalar(tmp4, esel[0], -3e38, None, ALU.mult))
                steps.step(V.tensor_tensor(tmp4, tmp4, sel, ALU.add))
                first_max(tmp4, top[1], esel[1], pick)
                V.tensor_tensor(pick, top[1], top[0], ALU.subtract).then_inc(gdiff.sem, 1)
                for k in range(2):
                    steps.mark(V.tensor_tensor(hot[k], gsel[:, :, :].rearrange("p n (g o) -> p n g o", o=1).to_broadcast([P, NT, EG, EG]),
                                               esel[k].rearrange("p n (o e) -> p n o e", o=1).to_broadcast([P, NT, EG, EG]), ALU.mult))
                steps.wait()
                hotf = [hot[k].rearrange("p n g e -> p n (g e)") for k in range(2)]
                V.tensor_tensor(both, hotf[0], hotf[1], ALU.add).then_inc(both_ready.sem, 1)
                dve.wait_ge(rank_mm.sem, rank_mm.at(l, 1))
                steps.mark(V.tensor_copy(rank, PS[1][:, 0:NT * E].rearrange("p (n e) -> p n e", n=NT)))
                steps.step(V.tensor_copy(count, PS[1][:, NT * E:NT * E + E]))
                flat = "p a b -> p (a b)"

                def spread(ap, pat, *shape, **kw):
                    return ap.rearrange(pat, **kw).to_broadcast(list(shape))

                for c in range(1, MAXC):
                    steps.mark(V.tensor_scalar(over[:, c - 1, :], count, float(c * P), None, ALU.is_gt))
                steps.wait()
                steps.step(V.tensor_tensor_scan(pos[:, 1:, :].rearrange(flat), ones48.rearrange(flat), over.rearrange(flat), float(E - 1), ALU.mult, ALU.add))
                steps.step(V.tensor_tensor(hr[:, 0:NT, :], hotf[0], rank, ALU.mult))
                steps.step(V.tensor_tensor(hr[:, NT:2 * NT, :], hotf[1], rank, ALU.mult))
                steps.step(V.tensor_reduce(rk, hr, AX, ALU.add))
                steps.step(V.tensor_tensor(ge, spread(rk, "p (k o) -> p k o", P, 2 * NT, MAXC + 1, o=1), spread(limits, "p (o c) -> p o c", P, 2 * NT, MAXC + 1, o=1), ALU.is_ge))
                steps.mark(V.tensor_tensor(inblk, ge[:, :, 0:MAXC], ge[:, :, 1:MAXC + 1], ALU.subtract))
                steps.step(V.tensor_reduce(gadd, ge[:, :, 1:MAXC], AX, ALU.add))
                steps.mark(V.scalar_tensor_tensor(rk, gadd, float(-P), rk, ALU.mult, ALU.add))
                for k in range(2):
                    steps.mark(V.tensor_tensor(big[:, k * NT:(k + 1) * NT, :, :], spread(hotf[k], "p n (o e) -> p n o e", P, NT, MAXC, E, o=1),
                                               spread(pos, "p (o c) e -> p o c e", P, NT, MAXC, E, o=1), ALU.mult))
                steps.wait()
                steps.step(V.tensor_reduce(col4, big, AX, ALU.add))
                steps.step(V.tensor_tensor(col4, col4, inblk, ALU.mult))
                steps.step(V.tensor_reduce(col, col4, AX, ALU.add))
                steps.mark(V.tensor_tensor(rk_hot, spread(rk, "p (k o) -> p k o", P, 2 * NT, P, o=1), spread(seq, "p (o j) -> p o j", P, 2 * NT, P, o=1), ALU.is_equal))
                steps.step(V.tensor_tensor(col_hot, spread(col, "p (k o) -> p k o", P, 2 * NT, SLOTS, o=1),
                                           spread(seq[:, 0:SLOTS], "p (o c) -> p o c", P, 2 * NT, SLOTS, o=1), ALU.is_equal))
                V.tensor_tensor(col_what, spread(col_hot, "p k (o c) -> p k o c", P, 2 * NT, 4, SLOTS, o=1),
                                spread(what, "p k (s o) -> p k s o", P, 2 * NT, 4, SLOTS, o=1), ALU.mult).then_inc(hot_ready.sem, 1)
                steps.mark(V.tensor_scalar(nover, pos[:, MAXC - 1, E - 1:E], float(E - 1), None, ALU.subtract))
                steps.step(V.tensor_tensor(match.rearrange("p x c e -> p x (c e)"), spread(pos[:, 1:, :], "p (o c) e -> p o (c e)", P, XB, (MAXC - 1) * E, o=1),
                                           spread(xcols, "p (x o) -> p x o", P, XB, (MAXC - 1) * E, o=1), ALU.is_equal))
                steps.step(V.tensor_tensor(match.rearrange("p x c e -> p x (c e)"), match.rearrange("p x c e -> p x (c e)"),
                                           spread(over, "p (o c) e -> p o (c e)", P, XB, (MAXC - 1) * E, o=1), ALU.mult))
                steps.step(V.tensor_tensor(match.rearrange("p x c e -> p (x c) e"), match.rearrange("p x c e -> p (x c) e"),
                                           spread(eidx, "p (o e) -> p o e", P, XB * (MAXC - 1), E, o=1), ALU.mult))
                steps.step(V.tensor_reduce(blk_f, match.rearrange("p x c e -> p x (c e)"), AX, ALU.add))
                steps.mark(V.tensor_copy(blk_e[:, 0:E], eidx))
                steps.mark(V.tensor_copy(blk_e[:, E:E + XB], blk_f))
                for q in range(4):
                    steps.mark(V.tensor_scalar(half4[:, q:q + 1], nover, float(2 * q), None, ALU.is_gt))
                    steps.mark(V.tensor_scalar(parity[:, q:q + 1], nover, float(2 * q), None, ALU.is_equal))
                steps.wait()
                steps.mark(V.tensor_reduce(gadd[:, 0:1], parity, AX, ALU.add))
                steps.step(V.tensor_reduce(nover, half4, AX, ALU.add))
                steps.mark(V.tensor_copy(two_i[:, 0:1], gadd[:, 0:1]))
                steps.step(V.tensor_tensor(gadd[:, 1:2], gadd[:, 0:1], nover, ALU.add))
                steps.mark(V.tensor_scalar(two_i[:, 1:2], gadd[:, 1:2], float(E // 2 - 1), 16.0, ALU.add, ALU.mult))
                steps.mark(V.tensor_scalar(last_i[:, 1:2], nover, float(E // 2 - 2), None, ALU.add))
                V.tensor_scalar(last_i[:, 0:1], nover, float(E // 2 - 1), None, ALU.add).then_inc(routed.sem, 1)
                dve.wait_ge(slots_mm.sem, slots_mm.at(l, 1))
                steps.step(V.tensor_copy(found, PS[2][:, 0:4 * SLOTS].rearrange("p (s c) -> p s c", s=4)))
                steps.mark(V.scalar_tensor_tensor(src_f, found[:, 1, :], float(P), found[:, 2, :], ALU.mult, ALU.add))
                steps.step(V.tensor_scalar(found[:, 0, :], found[:, 0, :], float(-NOWHERE), float(NOWHERE), ALU.mult, ALU.add))
                steps.step(V.tensor_tensor(src_f, src_f, found[:, 0, :], ALU.add))
                steps.mark(V.tensor_copy(src_ids, src_f))
                V.scalar_tensor_tensor(slot_ids, found[:, 3, :], float(T), src_f, ALU.mult, ALU.add).then_inc(src_ready.sem, 1)
                dve.wait_ge(gexp_done.sem, gexp_done.at(l, 2))
                steps.mark(V.tensor_reduce(gsum, gexp, AX, ALU.add))
                steps.step(V.tensor_scalar(top[0], pick, 1.0, None, ALU.add))
                steps.step(V.tensor_tensor(gsum, gsum, top[0], ALU.mult))
                steps.step(V.reciprocal(wt[0], gsum))
                steps.step(V.tensor_tensor(wt[1], wt[0], pick, ALU.mult))

            def moe_dve(l):
                routing(l)
                two = dve.value_load(two_i[0:1, 0:1], min_val=0, max_val=1)
                last = dve.value_load(last_i[0:1, 0:1], min_val=E // 2 - 1, max_val=(E + XB) // 2 - 1)
                gain = vn[:, V_NORM[f"f{l}"]:V_NORM[f"f{l}"] + KT]

                def trail(raw, hi, lo, lead_done, done, m):
                    for q in range(2):
                        kts = slice(q * KT // 2, (q + 1) * KT // 2)
                        dve.wait_ge(lead_done, 2 * m + (q + 1))
                        V.tensor_tensor(lo[:, kts, :], raw[:, kts, :], hi[:, kts, :].bitcast(F32), ALU.subtract).then_inc(done, 1)

                def gate_trail(b, m):
                    trail(wg[b], wgh, wgl[b], gh_done[l], gl_done[l], m)

                def up_trail(b, m):
                    trail(wu[b], wuh, wul[b], uh_done[l], ul_done[l], m)

                def copy_xgT(b, n):
                    dve.wait_ge(xgT_mm[l][b], n)
                    for q in range(2):
                        ins = V.tensor_tensor(xgT[b][:, 4 * q:4 * q + 4, :], PS[5 + q][:, :].rearrange("p (a b) -> p a b", a=4),
                                              gain[:, 4 * q:4 * q + 4].rearrange("p (a o) -> p a o", o=1).to_broadcast([P, 4, P]), ALU.mult)
                    ins.then_inc(xgT_done[l][b], 1)

                def rows_trail(b, m):
                    dve.wait_ge(xh_done[l], m + 1)
                    V.tensor_tensor(xgl[b][:, :, :], xgT[b], xgh[b][:, :, :].bitcast(F32), ALU.subtract).then_inc(xl_done[l], 1)

                gate_trail(0, 0)
                for b in range(2):
                    copy_xgT(b, 1)
                for b in range(2):
                    rows_trail(b, b)
                up_trail(0, 0)

                def pair(i, more):
                    def hidden(b):
                        dve.wait_ge(sil_done[l], 2 * i + (b + 1))
                        dve.wait_ge(up_mm[l], 2 * i + (b + 1))
                        V.tensor_tensor(hid, PS[1][:, :], sil, ALU.mult).then_inc(hid_done[l], 1)

                    def copy_hidT(b):
                        dve.wait_ge(hT_mm[l], 2 * i + (b + 1))
                        if b == 1:
                            dve.wait_ge(down_mm[l], 2 * i + 1)
                        V.tensor_copy(hidT.rearrange("p a b -> p (a b)"), PS[2][:, :]).then_inc(hidT_done[l], 1)

                    if more:
                        gate_trail(1, 2 * i + 1)
                        hidden(0)
                        up_trail(1, 2 * i + 1)
                        copy_hidT(0)
                        copy_xgT(0, i + 2)
                        gate_trail(0, 2 * i + 2)
                        rows_trail(0, 2 * i + 2)
                        hidden(1)
                        copy_hidT(1)
                        up_trail(0, 2 * i + 2)
                        copy_xgT(1, i + 2)
                        rows_trail(1, 2 * i + 3)
                        dve.wait_ge(down_mm[l], 2 * i + 2)
                    else:
                        with dve.If(two > 0):
                            gate_trail(1, 2 * i + 1)
                        hidden(0)
                        with dve.If(two > 0):
                            up_trail(1, 2 * i + 1)
                        copy_hidT(0)
                        with dve.If(two > 0):
                            hidden(1)
                            copy_hidT(1)

                with dve.Fori(0, last) as i:
                    pair(i, True)
                pair(last, False)

            moe_dve(0)
            def trailing(s, m):
                dve.wait_ge(wh_done, m)
                V.tensor_tensor(wl[:, s, :], wraw[:, s, :], wh[:, s, :].bitcast(F32), ALU.subtract).then_inc(wl_done, 1)

            norm_dve("kv", lambda n: combined(n, 0))
            dve.wait_ge(att_const, 32)
            per = 2 * 5 + 2 * 1 + 2 * 1
            with dve.Fori(0, NP_HEADS) as i:
                steps.enter(i, per)
                for t in range(6):
                    tab = 2 if t < 3 else 0
                    src = PS[t % 2]
                    dve.wait_ge(unit_mm, 9 * i + (t + 1))
                    if t < 2:
                        dve.wait_ge(pairs_done, i + 1)
                    else:
                        dve.wait_ge(rope_done, 12 * i + 2 * (t - 1))
                    V.tensor_tensor(rope_ab[:, 2 * (t % 2), :], src[:, :], rope_t[:, tab, :], ALU.mult)
                    for q in range(4):
                        s, d = 32 * (q ^ 1), 32 * q
                        ins = V.tensor_tensor(rope_ab[d:d + 32, 2 * (t % 2) + 1, :], src[s:s + 32, :], rope_t[s:s + 32, tab + 1, :], ALU.mult)
                    ins.then_inc(rope_ab_done, 1)
                    trailing(t % NU, 9 * i + (t + NU + 1))
                trailing(0, 9 * i + (6 + NU + 1))

                def maxima(h):
                    dve.wait_ge(s1_mm, 8 * i + (4 * h + 1))
                    steps.mark(V.tensor_reduce(NM[:, 1:3], PS[4][:, :].rearrange("p (a b) -> p a b", a=2), AX, ALU.max, negate=True))
                    dve.wait_ge(s1_mm, 8 * i + (4 * h + 2))
                    steps.mark(V.tensor_reduce(NM[:, 0:1], PS[5][:, 0:P], AX, ALU.max, negate=True))
                    steps.mark(V.tensor_reduce(NM[:, 3:4], PS[5][:, P:3 * P], AX, ALU.max, negate=True))
                    for k in (2, 3):
                        dve.wait_ge(s1_mm, 8 * i + (4 * h + k + 1))
                        steps.mark(V.tensor_reduce(NM[:, 4 * k - 4:4 * k], PS[4 + k][:, :].rearrange("p (a b) -> p a b", a=4), AX, ALU.max, negate=True))
                    steps.wait()
                    V.tensor_tensor(NM[:, 4:8], NM[:, 4:8], NM[:, 8:12], ALU.min).then_inc(max_done, 1)

                def maxima_row(h):
                    dve.wait_ge(row_mm, 2 * i + (h + 1))
                    steps.step(V.tensor_copy(rowt[0:1, :], PS[0][0:1, :]))
                    one = "p (o t) -> p o t"
                    V.tensor_tensor(Qh[h][HEAD:HEAD + 1, :, :], PS[1][0:1, :].rearrange(one, o=1).to_broadcast([1, NG, T]),
                                    rowt[0:1, :].rearrange(one, o=1).to_broadcast([1, NG, T]), ALU.min).then_inc(row_done, 1)

                maxima(0)
                maxima_row(0)
                maxima(1)
                trailing(1, 9 * i + (7 + NU + 1))
                maxima_row(1)
                trailing(2, 9 * i + (8 + NU + 1))
                for h in range(2):
                    O = PS[3 - h]
                    dve.wait_ge(pv_mm, 2 * i + (h + 1))
                    inv = rope_ab[0:HEAD, h, :]
                    steps.step(V.reciprocal(inv, O[HEAD:P, :]))
                    V.tensor_tensor(oT[h * HEAD:(h + 1) * HEAD, bass.ds(i, 1), :].rearrange("p a b -> p (a b)"), O[0:HEAD, :], inv, ALU.mult).then_inc(oT_done, 1)
                dve.wait_ge(oT_done, 2 * i + 2)
                V.tensor_copy(tick[0:1, :], vn[0:1, 0:1]).then_inc(pairs_done, 1)
                steps.leave(NP_HEADS)
            for c in range(KT):
                dve.wait_ge(oTh_done, c + 1)
                V.tensor_tensor(HQl[:, c, :], oT[:, c, :], HQh[:, c, :].bitcast(F32), ALU.subtract).then_inc(oTl_done, 1)
            for m in range(9 * NP_HEADS + NU, 9 * NP_HEADS + KT):
                trailing(m % NU, m + 1)
            norm_dve("f1", lambda n: projected(n, wo_mm, "f1"))
            moe_dve(1)
            norm_dve("out", lambda n: combined(n, 1))

        @block.tensor
        def _(pe):
            M = nc.tensor

            def norm_pe(k):
                if k in ("f0", "f1"):
                    pe.wait_ge(x_upd.sem, x_upd.at(k, NT))
                for n in range(NT):
                    pe.wait_ge(xn_ready.sem, xn_ready.at(k, n + 1))
                    for kt in range(KT):
                        ins = M.transpose(PS[kt][:, n * P:(n + 1) * P], XN[k][:, n, kt::KT], ident[:, :])
                        if n == NT - 1:
                            ins.then_inc(xT_ready.sem, 1)

            def normed(k):
                n = Q_READY if k == "kv" else KT // 2
                pe.wait_ge(ht_act.sem, ht_act.at(k, n))
                pe.wait_ge(ht_dve.sem, ht_dve.at(k, n))

            pe.wait_ge(const_in, 48)
            norm_pe("a")
            normed("a")
            with pe.Fori(0, KT // 2) as i:
                for b in range(2):
                    pe.wait_ge(win_in[b], (i + 1) * 16)
                    pe.wait_ge(glu_done[b], i + 1)
                    for s in range(2):
                        for kt in range(KT):
                            ins = M.matmul(PS[2 * b + s][:, :], w_in_sb[b][:, kt, s, :], HT[:, kt, :], start=kt == 0, stop=kt == KT - 1)
                    ins.then_inc(u_mm[b], 1)
            pe.wait_ge(conv_init, 1)
            for c in range(KT):
                pe.wait_ge(conv_done[c % 2], c // 2 + 2)
                ins = M.matmul(PS[4][:, :], onesf, HTQ[:, c, :], start=c == 0, stop=c == KT - 1)
            ins.then_inc(mean_mm, 1)
            for c in range(KT):
                pe.wait_ge(ln_sq, c + 1)
                M.matmul(PS[5][:, :], onesf, lnsq[c % 2], start=c == 0, stop=c == KT - 1).then_inc(var_mm, 1)
            pe.wait_ge(lnvar_ready, 1)
            for c in range(KT):
                pe.wait_ge(silu_trail, c + 1)
                for n in range(NT):
                    hi, lo = HTh[:, c, n * P:(n + 1) * P], HTl[:, c, n * P:(n + 1) * P]
                    for h in range(2):
                        dst, cols = PS[2 * n + h][:, :], slice(h * 512, (h + 1) * 512)
                        M.matmul(dst, hi, WOh[:, c, cols], start=c == 0, stop=False)
                        M.matmul(dst, hi, WOl[:, c, cols], start=False, stop=False)
                        ins = M.matmul(dst, lo, WOh[:, c, cols], start=False, stop=c == KT - 1)
                        if c == KT - 1:
                            ins.then_inc(wout_mm, 1)

            def moe_pe(l):
                norm_pe(f"f{l}")
                normed(f"f{l}")
                pe.wait_ge(rt_in.sem, rt_in.at(l, 16))
                for n in range(NT):
                    for kt in range(KT):
                        ins = M.matmul(PS[0][:, n * (EG + E):(n + 1) * (EG + E)], HT[:, kt, n * P:(n + 1) * P], rt[:, kt, :],
                                       start=kt == 0, stop=kt == KT - 1)
                ins.then_inc(logit_mm.sem, 1)
                pe.wait_ge(both_ready.sem, both_ready.at(l, 1))
                for n in range(NT + 1):
                    for m in range(min(n + 1, NT)):
                        ins = M.matmul(PS[1][:, n * E:(n + 1) * E], before_b if m == n else ones_b, both[:, m, :],
                                       start=m == 0, stop=m == min(n, NT - 1))
                ins.then_inc(rank_mm.sem, 1)
                pe.wait_ge(hot_ready.sem, hot_ready.at(l, 1))
                for k in range(2 * NT):
                    ins = M.matmul(PS[2][:, 0:4 * SLOTS], rk_hot[:, k, :], col_what[:, k, :, :].rearrange("p s c -> p (s c)"),
                                   start=k == 0, stop=k == 2 * NT - 1)
                ins.then_inc(slots_mm.sem, 1)
                pe.wait_ge(routed.sem, routed.at(l, 1))
                two = pe.value_load(two_i[0:1, 0:1], min_val=0, max_val=1)
                last = pe.value_load(last_i[0:1, 0:1], min_val=E // 2 - 1, max_val=(E + XB) // 2 - 1)

                def transpose_rows(b, n):
                    pe.wait_ge(gathered[l][b], n * 16)
                    if b == 1 or not isinstance(n, int):
                        pe.wait_ge(xgT_done[l][1 - b], n - 1 if b == 0 else n)
                    for kt in range(KT):
                        ins = M.transpose(PS[5 + kt // 4][:, (kt % 4) * P:(kt % 4 + 1) * P], xg[b][:, kt::KT], ident[:, :])
                    ins.then_inc(xgT_mm[l][b], 1)

                for b in range(2):
                    transpose_rows(b, 1)

                def project(dst, b, m, hi, lo, ready):
                    pe.wait_ge(xl_done[l], m + 1)
                    for kt in range(KT):
                        if kt % (KT // 2) == 0:
                            pe.wait_ge(ready, 2 * m + (kt // (KT // 2) + 1))
                        M.matmul(dst, xgh[b][:, kt, :], hi[:, kt, :], start=kt == 0, stop=False)
                        M.matmul(dst, xgh[b][:, kt, :], lo[:, kt, :], start=False, stop=False)
                        ins = M.matmul(dst, xgl[b][:, kt, :], hi[:, kt, :], start=False, stop=kt == KT - 1)
                    return ins

                def pair(i, more):
                    def gate(b):
                        if b == 1:
                            pe.wait_ge(sil_done[l], 2 * i + 1)
                        project(PS[0][:, :], b, 2 * i + b, wgh, wgl[b], gl_done[l]).then_inc(gate_mm[l], 1)

                    def up(b):
                        project(PS[1][:, :], b, 2 * i + b, wuh, wul[b], ul_done[l]).then_inc(up_mm[l], 1)

                    def transpose_hidden(b):
                        pe.wait_ge(hid_done[l], 2 * i + (b + 2))
                        for ft in range(FT):
                            ins = M.transpose(PS[2][:, ft * P:(ft + 1) * P], hid[:, ft::FT], ident[:, :])
                        ins.then_inc(hT_mm[l], 1)

                    def down(b):
                        pe.wait_ge(wd_in[l][b], (i + 1) * 16)
                        pe.wait_ge(hidT_done[l], 2 * i + (b + 1))
                        pe.wait_ge(y_done[l], 2 * i + (b + 1))
                        for h in range(2):
                            for ft in range(FT):
                                ins = M.matmul(PS[3 + h][:, :], hidT[:, ft, :], wd[b][:, ft, h * 512:(h + 1) * 512],
                                               start=ft == 0, stop=ft == FT - 1)
                        ins.then_inc(down_mm[l], 1)

                    gate(0)
                    up(0)
                    if more:
                        gate(1)
                        transpose_hidden(0)
                        transpose_rows(0, i + 2)
                        up(1)
                        down(0)
                        transpose_hidden(1)
                        transpose_rows(1, i + 2)
                        down(1)
                    else:
                        with pe.If(two > 0):
                            gate(1)
                        transpose_hidden(0)
                        with pe.If(two > 0):
                            up(1)
                        down(0)
                        with pe.If(two > 0):
                            transpose_hidden(1)
                            down(1)

                with pe.Fori(0, last) as i:
                    pair(i, True)
                pair(last, False)

            moe_pe(0)
            norm_pe("kv")
            normed("kv")
            pe.wait_ge(att_const, 32)
            pe.wait_ge(att_init, 1)

            with pe.Fori(0, NP_HEADS) as i:
                def tile_of(g, n):
                    return slice(n * P, (n + 1) * P) if g == 0 else slice(n, T, NT)

                for t in range(6):
                    hi, lo, g = (HQh, HQl, t) if t < 3 else (HTh, HTl, t - 3)
                    if t == 3:
                        pe.wait_ge(ht_act.sem, ht_act.at("kv", 2 * KT))
                        pe.wait_ge(ht_dve.sem, ht_dve.at("kv", 2 * KT))
                    pe.wait_ge(wl_done, 9 * i + (t + 1))
                    if t < 2:
                        pe.wait_ge(row_done, 2 * i + 1)
                    else:
                        pe.wait_ge(rope_ab_done, 6 * i + (t - 1))
                    for kt in range(KT):
                        whk, wlk = wh[:, t % NU, kt * P:(kt + 1) * P], wl[:, t % NU, kt * P:(kt + 1) * P]
                        M.matmul(PS[t % 2][:, :], whk, hi[:, kt, :], start=kt == 0, stop=False)
                        M.matmul(PS[t % 2][:, :], whk, lo[:, kt, :], start=False, stop=False)
                        ins = M.matmul(PS[t % 2][:, :], wlk, hi[:, kt, :], start=False, stop=kt == KT - 1)
                    ins.then_inc(unit_mm, 1)

                def values(g):
                    pe.wait_ge(wl_done, 9 * i + (7 + g))
                    if g == 0:
                        pe.wait_ge(pairs_done, i + 1)
                    if g == 2:
                        pe.wait_ge(v_done, 3 * i + 1)
                    dst = PS[2 + g % 2][:, :]
                    for kt in range(KT):
                        whk, wlk = wh[:, g, kt * P:(kt + 1) * P], wl[:, g, kt * P:(kt + 1) * P]
                        M.matmul(dst, whk, HTh[:, kt, :], start=kt == 0, stop=False)
                        M.matmul(dst, whk, HTl[:, kt, :], start=False, stop=False)
                        ins = M.matmul(dst, wlk, HTh[:, kt, :], start=False, stop=kt == KT - 1)
                    ins.then_inc(unit_mm, 1)

                def turn(g):
                    pe.wait_ge(vT_done, 3 * i + (g + 1))
                    for n in range(NT):
                        ins = M.transpose(PS[2 + g % 2][:, n * P:(n + 1) * P], vT[:, tile_of(g, n)], ident[:, :])
                    ins.then_inc(v_mm, 1)

                def lay_mask(bank, blocks):
                    if len(set(blocks)) == 1:
                        M.matmul(PS[bank][:, :], ident_b, masks_b[:, blocks[0]:blocks[0] + 1, :].to_broadcast([P, 4, P]), start=True, stop=False)
                    else:
                        for j, m in enumerate(blocks):
                            M.matmul(PS[bank][:, j * P:(j + 1) * P], ident_b, masks_b[:, m, :], start=j == 0, stop=False)

                def scores(h):
                    if h == 0:
                        pe.wait_ge(pairs_done, i + 1)
                    else:
                        pe.wait_ge(max_done, 2 * i + 1)
                    pe.wait_ge(hi_done, 2 * i + (h + 1))
                    q, k = QKh[:, 0, :, :], QKh[:, 1, :, :]
                    for s, (mask, parts) in enumerate((
                            ([PREV, OWN, PREV, OWN], [(0, 1, 0, 256), (0, 2, 256, 256)]),
                            ([OWN, PREV, OWN], [(0, 0, 0, 128), (0, 3, 128, 256)]),
                            ([OWN] * 4, [(1, n, n * P, 128) for n in range(NT)]),
                            ([PHASE] * 4, [(2, n, n * P, 128) for n in range(NT)]))):
                        lay_mask(4 + s, mask)
                        for j, (g, n, at, w) in enumerate(parts):
                            keys = slice((n + 1) * P - w, (n + 1) * P) if g == 0 else tile_of(g, n)
                            ins = M.matmul(PS[4 + s][:, at:at + w], q[0:HEAD, g, tile_of(g, n)], k[0:HEAD, g, keys],
                                           start=False, stop=j == len(parts) - 1)
                        ins.then_inc(s1_mm, 1)

                def max_rows(h):
                    pe.wait_ge(max_done, 2 * i + (h + 1))
                    if h == 1:
                        pe.wait_ge(row_done, 2 * i + 2)
                    for n in range(NT):
                        M.transpose(PS[0][0:1, n * P:(n + 1) * P], NM[:, n:n + 1], ident[:, :])
                    for n in range(NT):
                        ins = M.transpose(PS[1][0:1, n::NT], NM[:, NT + n:NT + n + 1], ident[:, :])
                    ins.then_inc(row_mm, 1)

                def scores_t(h):
                    pe.wait_ge(row_done, 2 * i + (h + 2))
                    q, k = Qh[h], Kh[h]
                    for s, (mask, parts) in enumerate((
                            ([OWN_T] * 4, [(1, n, n * P, 128) for n in range(NT)]),
                            ([PHASE_T] * 4, [(2, n, n * P, 128) for n in range(NT)]),
                            ([OWN_T, PREV_T, OWN_T, PREV_T], [(0, 0, 0, 256), (0, 1, 256, 256)]),
                            ([OWN_T, PREV_T, OWN_T], [(0, 2, 0, 256), (0, 3, 256, 128)]))):
                        if h == 0:
                            pe.wait_ge(max_done, 2 * i + 2)
                        else:
                            pe.wait_ge(exp_done, 8 * i + (s + 1))
                        lay_mask(4 + s, mask)
                        for j, (g, n, at, w) in enumerate(parts):
                            queries = slice(n * P, n * P + w) if g == 0 else tile_of(g, n)
                            ins = M.matmul(PS[4 + s][:, at:at + w], k[0:HEAD + 1, g, tile_of(g, n)], q[0:HEAD + 1, g, queries],
                                           start=False, stop=j == len(parts) - 1)
                        ins.then_inc(s2_mm, 1)

                def weigh(h):
                    pe.wait_ge(v_done, 3 * i + 3)
                    O = PS[3 - h]
                    for s, parts in enumerate((
                            [(1, n, n * P, 128) for n in range(NT)],
                            [(2, n, n * P, 128) for n in range(NT)],
                            [(0, 0, 0, 256), (0, 1, 256, 256)],
                            [(0, 2, 0, 256), (0, 3, 256, 128)])):
                        pe.wait_ge(exp_done, 8 * i + (4 * h + s + 1))
                        for g, n, at, w in parts:
                            queries = slice(n * P, n * P + w) if g == 0 else tile_of(g, n)
                            ins = M.matmul(O[:, queries], Vs[:, g, n, h, :], Pm[h][:, s * 512 + at:s * 512 + at + w],
                                           start=s == 0 and n == 0, stop=s == 3 and n == 3)
                    ins.then_inc(pv_mm, 1)

                values(0)
                scores(0)
                turn(0)
                values(1)
                max_rows(0)
                scores(1)
                turn(1)
                values(2)
                max_rows(1)
                turn(2)
                scores_t(0)
                scores_t(1)
                weigh(0)
                weigh(1)
            pe.wait_ge(pairs_done, NP_HEADS + 1)
            for c in range(KT):
                u = (9 * NP_HEADS + c) % NU
                pe.wait_ge(wl_done, 9 * NP_HEADS + c + 1)
                pe.wait_ge(oTl_done, c + 1)
                for n in range(NT):
                    tok_n = slice(n * P, (n + 1) * P)
                    for h in range(2):
                        cols = slice(h * 512, (h + 1) * 512)
                        dst = PS[2 * n + h][:, :]
                        M.matmul(dst, HQh[:, c, tok_n], wh[:, u, cols], start=c == 0, stop=False)
                        M.matmul(dst, HQh[:, c, tok_n], wl[:, u, cols], start=False, stop=False)
                        ins = M.matmul(dst, HQl[:, c, tok_n], wh[:, u, cols], start=False, stop=c == KT - 1)
                        if c == KT - 1:
                            ins.then_inc(wo_mm, 1)
                if c < KT - 1:
                    ins.then_inc(unit_mm, 1)
            moe_pe(1)


def bf16_bits(x):
    import numpy as np
    return (np.ascontiguousarray(x, np.float32).view(np.uint32) >> 16).astype(np.uint16)


def constants():
    import numpy as np
    i, j = np.arange(P)[:, None], np.arange(P)[None, :]
    ident = np.eye(P, dtype=np.float32)
    c16 = bf16_bits(np.concatenate([ident, (i < j).astype(np.float32), np.ones((P, P), np.float32)], 1))
    no = np.float32(-BIG)
    own = np.where(j <= i, np.float32(0), no)
    prev = np.where(j >= i, np.float32(0), no)
    phase = np.where((i - j) % 4 == 0, own, no)
    masks = bf16_bits(np.concatenate([prev, own, phase, own.T, prev.T, phase.T], 1))
    pos = np.arange(T, dtype=np.float32)
    inv = np.float32(10000.0) ** (-np.arange(0, HEAD, 2, dtype=np.float32) / np.float32(HEAD))
    ang = (inv[:, None] * pos[None, :]).astype(np.float32)
    cos = np.tile(np.cos(ang), (4, 1)).astype(np.float32)
    sin = np.tile(np.sin(ang), (4, 1)).astype(np.float32)
    sign = np.where((np.arange(P) // 32) % 2 == 0, np.float32(1), np.float32(-1))[:, None]
    scale = np.float32(HEAD ** -0.5)
    rope = np.stack([cos, sin * sign, cos * scale, sin * sign * scale], 1)
    return {"ident": ident, "c16": c16, "masks": masks, "rope": np.ascontiguousarray(rope, np.float32)}


def lay_out(i):
    import numpy as np
    f = {k: np.asarray(v) for k, v in i.items()}
    cat, asc = np.concatenate, np.ascontiguousarray
    by_row = lambda v: v.reshape(P, KT)
    by_tile = lambda v: v.reshape(-1, P).T
    a = {"x": f["x"]}
    a["norm_vecs"] = asc(cat([by_row(f["a_norm"][0]), by_row(f["ffn_norm"][0]), by_row(f["kv_norm"]),
                              by_row(f["b_norm"][0]), by_row(f["ffn_norm"][1])], 1))
    a["conv_vecs"] = asc(cat([by_tile(f["a_b_in"][0]), by_tile(f["a_b_dw"][0]), by_tile(f["a_ln_g"][0]), by_tile(f["a_ln_b"][0]),
                              f["a_w_dw"][0].reshape(CONV, KT, P).transpose(2, 1, 0).reshape(P, KT * CONV)], 1))
    a["w_in"] = asc(f["a_w_in"][0].reshape(P, KT, 2, KT, P).transpose(3, 0, 1, 2, 4).reshape(KT, P, KT * 2 * P))
    a["w_out"] = f["a_w_out"][0].reshape(KT, P, D)
    a["b_out"] = f["a_b_out"][0].reshape(1, D)
    kv = f["w_kv"].reshape(P, KT, 2, NG, NP_HEADS, P)
    q = f["b_w_q"][0].reshape(P, KT, NG, NP_HEADS, P)
    a["w_qkv"] = asc(np.stack([q, kv[:, :, 0], kv[:, :, 1]]).transpose(4, 0, 3, 1, 2, 5).reshape(NP_HEADS * 9, P, KT * P))
    a["w_o"] = f["b_w_o"][0].reshape(KT, P, D)
    a["router"] = asc(cat([f["router_group"], f["router_expert"].transpose(0, 2, 1, 3).reshape(2, D, E)], 2)
                      .reshape(2, P, KT * (EG + E)))
    for k in ("w_gate", "w_up", "w_down"):
        a[k] = f[k].reshape(2 * E, P, -1)
    a["final_norm"] = f["final_norm"].reshape(1, D)
    return a


def kernel(**inputs):
    import concourse.bacc as bacc
    from concourse.bass_utils import run_bass_kernel_spmd

    nc = bacc.Bacc("TRN2", target_bir_lowering=False, num_devices=1)
    arrays = {**lay_out(inputs), **constants()}
    aps = {n: nc.dram_tensor(n, v.shape, mybir.dt.from_np(v.dtype), kind="ExternalInput").ap() for n, v in arrays.items()}
    aps["w_out"] = aps["w_out"].rearrange("c p n -> p c n")
    aps["out"] = nc.dram_tensor("out", (1, T, D), F32, kind="ExternalOutput").ap()
    build_program(nc, aps)
    r = run_bass_kernel_spmd(nc, [arrays], core_ids=[0])
    return r.results[0]["out"]
```
